# Optimizing a Trainium2 kernel written in Bass

```python
import functools
import jax
import jax.numpy as jnp
from jax import lax
import numpy as np

D_MODEL = 1024
BATCH = 1
SEQ = 128
DEPTH = 2
DEC_BATCH = 1
DEC_SEQ = 256
PAST_LEN = 128

GRID_W = 64
N_AB_LAYERS = (DEPTH + 1) // 2
N_NA_LAYERS = DEPTH // 2
A_HEADS = 8
A_KV_HEADS = 2
A_HEAD_DIM = 64
A_WIDTH = A_HEADS * A_HEAD_DIM
A_KV_WIDTH = A_KV_HEADS * A_HEAD_DIM
B_HEADS = 4
B_HEAD_DIM = 128
B_WIDTH = B_HEADS * B_HEAD_DIM
MLSTM_CHUNK = 128
AB_SIZES = (A_WIDTH, A_KV_WIDTH, A_KV_WIDTH, B_WIDTH, B_WIDTH, B_WIDTH, B_WIDTH, 4 * B_HEADS)
AB_IN_WIDTH = A_WIDTH + 2 * A_KV_WIDTH + 4 * B_WIDTH + 4 * B_HEADS
AB_OUT_WIDTH = A_WIDTH + B_WIDTH
C_HEADS = 16
C_HEAD_DIM = 64
C_WIDTH = C_HEADS * C_HEAD_DIM
NA_ROWS_MAX = 8
NA_COLS = 16
N_GROUPS = 4
EXPERTS_PER_GROUP = 8
N_EXPERTS = N_GROUPS * EXPERTS_PER_GROUP
TOP_K_IN_GROUP = 2
D_EXPERT = 512
MOE_BLOCK = 128
QUERY_BLOCK = 128
ROPE_BASE = 10000.0
NORM_EPS = 1e-6

kernel_name = "hybrid_dit_gqa_mlstm_natten_hmoe_step"

def rms_norm(x, g):
    xf = x.astype(jnp.float32)
    y = xf * lax.rsqrt(jnp.mean(xf * xf, axis=-1, keepdims=True) + NORM_EPS)
    return (y * g.astype(jnp.float32)).astype(x.dtype)

def axial_rope(x):
    n, d = x.shape[1], x.shape[-1]
    half = d // 2
    t = jnp.arange(n)
    row = (t // GRID_W).astype(jnp.float32)
    col = (t % GRID_W).astype(jnp.float32)
    freqs = 1.0 / (ROPE_BASE ** (jnp.arange(0, half, 2, dtype=jnp.float32) / half))

    def rot(xh, pos):
        ang = pos[:, None] * freqs[None, :]
        cos = jnp.cos(ang)[None, :, None, :]
        sin = jnp.sin(ang)[None, :, None, :]
        x1, x2 = jnp.split(xh, 2, axis=-1)
        return jnp.concatenate([x1 * cos - x2 * sin, x1 * sin + x2 * cos], axis=-1)

    xf = x.astype(jnp.float32)
    out = jnp.concatenate([rot(xf[..., :half], row), rot(xf[..., half:], col)], axis=-1)
    return out.astype(x.dtype)

def blocked_attention(q, k, v):
    b, n, hq, d = q.shape
    hkv = k.shape[2]
    g = hq // hkv
    scale = d ** -0.5
    qb = q.reshape(b, n // QUERY_BLOCK, QUERY_BLOCK, hkv, g, d).transpose(1, 0, 2, 3, 4, 5)

    def one_block(qi):
        s = jnp.einsum('bqkgd,btkd->bkgqt', qi, k).astype(jnp.float32) * scale
        p = jax.nn.softmax(s, axis=-1).astype(v.dtype)
        return jnp.einsum('bkgqt,btkd->bqkgd', p, v)

    o = lax.map(one_block, qb)
    return o.transpose(1, 0, 2, 3, 4, 5).reshape(b, n, hq, d)

def neighbourhood_attention(q, k, v, ctx_k, ctx_v, rpb):
    b, n, hh, d = q.shape
    rows = n // GRID_W
    kr = min(NA_ROWS_MAX, rows)
    kc = NA_COLS
    scale = d ** -0.5
    kg = k.reshape(b, rows, GRID_W, hh, d)
    vg = v.reshape(b, rows, GRID_W, hh, d)
    qg = jnp.moveaxis(q.reshape(b, rows, GRID_W, hh, d), 1, 0)
    r_idx = jnp.arange(rows)
    row_start = jnp.clip(r_idx - kr // 2, 0, rows - kr)
    cols = jnp.arange(GRID_W)
    col_start = jnp.clip(cols - kc // 2, 0, GRID_W - kc)
    col_idx = col_start[:, None] + jnp.arange(kc)[None, :]
    dcol = col_idx - cols[:, None] + (NA_COLS - 1)

    def one_row(args):
        qr, r, rs = args
        kb = lax.dynamic_slice_in_dim(kg, rs, kr, axis=1)
        vb = lax.dynamic_slice_in_dim(vg, rs, kr, axis=1)
        kw = kb[:, :, col_idx]
        vw = vb[:, :, col_idx]
        drow = rs + jnp.arange(kr) - r + (NA_ROWS_MAX - 1)
        bias = rpb[:, drow][:, :, dcol]
        bias = jnp.transpose(bias, (0, 2, 1, 3)).reshape(hh, GRID_W, kr * kc)
        s_win = jnp.einsum('bqhd,brqjhd->bhqrj', qr, kw).astype(jnp.float32)
        s_win = s_win.reshape(b, hh, GRID_W, kr * kc) * scale + bias.astype(jnp.float32)
        s_ctx = jnp.einsum('bqhd,bphd->bhqp', qr, ctx_k).astype(jnp.float32) * scale
        p = jax.nn.softmax(jnp.concatenate([s_win, s_ctx], axis=-1), axis=-1).astype(v.dtype)
        p_win = p[..., :kr * kc].reshape(b, hh, GRID_W, kr, kc)
        p_ctx = p[..., kr * kc:]
        return (jnp.einsum('bhqrj,brqjhd->bqhd', p_win, vw)
                + jnp.einsum('bhqp,bphd->bqhd', p_ctx, ctx_v))

    o = lax.map(one_row, (qg, r_idx, row_start))
    return jnp.moveaxis(o, 0, 1).reshape(b, n, hh, d)

def mlstm_scan(q, k, v, i_pre, f_pre, c0, n0, m0):
    b, n, h, d = q.shape
    nc = n // MLSTM_CHUNK
    L = MLSTM_CHUNK

    def chunks(x):
        x = x.astype(jnp.float32).reshape((b, nc, L, h) + x.shape[3:])
        return jnp.swapaxes(jnp.moveaxis(x, 1, 0), 2, 3)

    qc = chunks(q)
    kc = chunks(k) * (d ** -0.5)
    vc = chunks(v)
    li = chunks(i_pre)
    lf = jax.nn.log_sigmoid(chunks(f_pre))
    causal = jnp.tril(jnp.ones((L, L), dtype=bool))

    def step(carry, inp):
        C, nv, m = carry
        qx, kx, vx, lix, lfx = inp
        bcum = jnp.cumsum(lfx, axis=-1)
        dlog = jnp.where(causal, bcum[..., :, None] - bcum[..., None, :] + lix[..., None, :], -jnp.inf)
        inter = bcum + m[..., None]
        m_t = jnp.maximum(inter, jnp.max(dlog, axis=-1))
        w_in = jnp.exp(dlog - m_t[..., None])
        w_st = jnp.exp(inter - m_t)
        a = jnp.einsum('bhtd,bhsd->bhts', qx, kx) * w_in
        num = (w_st[..., None] * jnp.einsum('bhtd,bhde->bhte', qx, C)
               + jnp.einsum('bhts,bhse->bhte', a, vx))
        den = w_st * jnp.einsum('bhtd,bhd->bht', qx, nv) + jnp.sum(a, axis=-1)
        hx = num / jnp.maximum(jnp.abs(den), jnp.exp(-m_t))[..., None]
        b_end = bcum[..., -1]
        log_ws = b_end[..., None] - bcum + lix
        m_new = jnp.maximum(b_end + m, jnp.max(log_ws, axis=-1))
        ws = jnp.exp(log_ws - m_new[..., None])
        wc = jnp.exp(b_end + m - m_new)
        C_new = wc[..., None, None] * C + jnp.einsum('bhs,bhsd,bhse->bhde', ws, kx, vx)
        n_new = wc[..., None] * nv + jnp.einsum('bhs,bhsd->bhd', ws, kx)
        return (C_new, n_new, m_new), hx

    carry0 = (c0.astype(jnp.float32), n0.astype(jnp.float32), m0.astype(jnp.float32))
    (cT, nT, mT), hs = lax.scan(step, carry0, (qc, kc, vc, li, lf))
    hs = jnp.moveaxis(jnp.swapaxes(hs, 2, 3), 0, 1).reshape(b, n, h, d)
    return hs, cT, nT, mT

def mlstm_bidir(q, k, v, gates, c0, n0, m0):
    hf, cf, nf, mf = mlstm_scan(q, k, v, gates[:, :, 0], gates[:, :, 1], c0[:, 0], n0[:, 0], m0[:, 0])
    flip = lambda x: jnp.flip(x, axis=1)
    hb, cb, nb, mb = mlstm_scan(flip(q), flip(k), flip(v), flip(gates[:, :, 2]), flip(gates[:, :, 3]),
                                c0[:, 1], n0[:, 1], m0[:, 1])
    h = hf + flip(hb)
    return h, jnp.stack([cf, cb], axis=1), jnp.stack([nf, nb], axis=1), jnp.stack([mf, mb], axis=1)

def ab_mixer(w_in, w_out, q_norm, k_norm, gate_bias, out_norm, h, ctx=None):
    b, n, _ = h.shape
    split_idx = [int(s) for s in np.cumsum(AB_SIZES)[:-1]]
    aq, ak, av, bq, bk, bv, bo, bg = jnp.split(h @ w_in, split_idx, axis=-1)
    aq = rms_norm(aq.reshape(b, n, A_HEADS, A_HEAD_DIM), q_norm)
    ak = rms_norm(ak.reshape(b, n, A_KV_HEADS, A_HEAD_DIM), k_norm)
    av = av.reshape(b, n, A_KV_HEADS, A_HEAD_DIM)
    bq = bq.reshape(b, n, B_HEADS, B_HEAD_DIM)
    bk = bk.reshape(b, n, B_HEADS, B_HEAD_DIM)
    bv = bv.reshape(b, n, B_HEADS, B_HEAD_DIM)
    gates = bg.reshape(b, n, 4, B_HEADS) + gate_bias
    if ctx is None:
        a_out = blocked_attention(aq, ak, av)
        c0 = jnp.zeros((b, 2, B_HEADS, B_HEAD_DIM, B_HEAD_DIM), jnp.float32)
        n0 = jnp.zeros((b, 2, B_HEADS, B_HEAD_DIM), jnp.float32)
        m0 = jnp.zeros((b, 2, B_HEADS), jnp.float32)
    else:
        ctx_k, ctx_v, c0, n0, m0 = ctx
        aq, ak = axial_rope(aq), axial_rope(ak)
        a_out = blocked_attention(aq, jnp.concatenate([ctx_k, ak], axis=1),
                                  jnp.concatenate([ctx_v, av], axis=1))
    hm, cT, nT, mT = mlstm_bidir(bq, bk, bv, gates, c0, n0, m0)
    b_out = rms_norm(hm, out_norm).astype(h.dtype) * jax.nn.sigmoid(bo.reshape(b, n, B_HEADS, B_HEAD_DIM))
    out = jnp.concatenate([a_out.reshape(b, n, A_WIDTH), b_out.reshape(b, n, B_WIDTH)], axis=-1) @ w_out
    if ctx is None:
        return out, (ak, av, cT, nT, mT)
    return out, ()

def na_mixer(w_in, w_out, rpb, h, ctx=None):
    b, n, _ = h.shape
    q, k, v = jnp.split(h @ w_in, 3, axis=-1)
    q = q.reshape(b, n, C_HEADS, C_HEAD_DIM)
    k = k.reshape(b, n, C_HEADS, C_HEAD_DIM)
    v = v.reshape(b, n, C_HEADS, C_HEAD_DIM)
    if ctx is None:
        o = blocked_attention(q, k, v)
        state = (k, v)
    else:
        o = neighbourhood_attention(q, k, v, ctx[0], ctx[1], rpb)
        state = ()
    return o.reshape(b, n, C_WIDTH) @ w_out, state

def hier_moe(x, wg, bg, we, be, w1, w3, w2):
    b, n, dm = x.shape
    t = b * n
    xt = x.reshape(t, dm)
    g_logits = (xt @ wg + bg).astype(jnp.float32)
    g_sel = jnp.argmax(g_logits, axis=-1)
    g_prob = jnp.take_along_axis(jax.nn.softmax(g_logits, axis=-1), g_sel[:, None], axis=1)[:, 0]
    e_logits = (xt @ we + be).astype(jnp.float32).reshape(t, N_GROUPS, EXPERTS_PER_GROUP)
    e_logits = jnp.take_along_axis(e_logits, g_sel[:, None, None], axis=1)[:, 0]
    top_v, top_i = lax.top_k(e_logits, TOP_K_IN_GROUP)
    weights = (jax.nn.softmax(top_v, axis=-1) * g_prob[:, None]).reshape(-1)
    eid = (g_sel[:, None] * EXPERTS_PER_GROUP + top_i).reshape(-1).astype(jnp.int32)
    tok = jnp.repeat(jnp.arange(t, dtype=jnp.int32), TOP_K_IN_GROUP)
    onehot = (eid[:, None] == jnp.arange(N_EXPERTS, dtype=jnp.int32)[None, :]).astype(jnp.int32)
    rank = jnp.take_along_axis(jnp.cumsum(onehot, axis=0), eid[:, None], axis=1)[:, 0] - 1
    counts = jnp.sum(onehot, axis=0)
    padded = (counts + MOE_BLOCK - 1) // MOE_BLOCK * MOE_BLOCK
    seg_end = jnp.cumsum(padded)
    seg_start = seg_end - padded
    dest = seg_start[eid] + rank
    n_blocks = (t * TOP_K_IN_GROUP + N_EXPERTS * (MOE_BLOCK - 1) + MOE_BLOCK - 1) // MOE_BLOCK
    cap = n_blocks * MOE_BLOCK
    slot_tok = jnp.full((cap,), t, dtype=jnp.int32).at[dest].set(tok)
    slot_w = jnp.zeros((cap,), x.dtype).at[dest].set(weights.astype(x.dtype))
    block_expert = jnp.minimum(
        jnp.searchsorted(seg_end, jnp.arange(n_blocks, dtype=jnp.int32) * MOE_BLOCK, side='right'),
        N_EXPERTS - 1)
    x_pad = jnp.concatenate([xt, jnp.zeros((1, dm), xt.dtype)], axis=0)
    xb = x_pad[slot_tok].reshape(n_blocks, MOE_BLOCK, dm)

    def expert_block(args):
        xi, e = args
        hid = jax.nn.silu(xi @ w1[e]) * (xi @ w3[e])
        return hid @ w2[e]

    yb = lax.map(expert_block, (xb, block_expert)).reshape(cap, dm)
    y = jax.ops.segment_sum(yb * slot_w[:, None], slot_tok, num_segments=t + 1)[:t]
    return y.reshape(b, n, dm)

def adaln_layer(x, cond, g_mix, g_ffn, ada_w, ada_b, mixer, moe_params):
    mod = (jax.nn.silu(cond) @ ada_w + ada_b)[:, None, :]
    sh1, sc1, g1, sh2, sc2, g2 = jnp.split(mod, 6, axis=-1)
    out, state = mixer(rms_norm(x, g_mix) * (1 + sc1) + sh1)
    x = x + g1 * out
    x = x + g2 * hier_moe(rms_norm(x, g_ffn) * (1 + sc2) + sh2, *moe_params)
    return x, state

def setup_inputs(seed: int = 0) -> dict:
    key = jax.random.key(seed)
    ks = jax.random.split(key, 40)
    nrm = lambda i, shape, s: jax.random.normal(ks[i], shape, jnp.float32) * s
    D = D_MODEL
    return {
        "x_prompt": nrm(0, (BATCH, SEQ, D), 1.0),
        "x_sample": nrm(1, (DEC_BATCH, DEC_SEQ, D), 1.0),
        "cache_attn_k": nrm(2, (DEC_BATCH, N_AB_LAYERS, PAST_LEN, A_KV_HEADS, A_HEAD_DIM), 1.0),
        "cache_attn_v": nrm(3, (DEC_BATCH, N_AB_LAYERS, PAST_LEN, A_KV_HEADS, A_HEAD_DIM), 1.0),
        "state_mlstm_C": nrm(4, (DEC_BATCH, N_AB_LAYERS, 2, B_HEADS, B_HEAD_DIM, B_HEAD_DIM), 0.1),
        "state_mlstm_n": nrm(5, (DEC_BATCH, N_AB_LAYERS, 2, B_HEADS, B_HEAD_DIM), 0.1),
        "state_mlstm_m": nrm(6, (DEC_BATCH, N_AB_LAYERS, 2, B_HEADS), 0.5),
        "cache_na_k": nrm(7, (DEC_BATCH, N_NA_LAYERS, PAST_LEN, C_HEADS, C_HEAD_DIM), 1.0),
        "cache_na_v": nrm(8, (DEC_BATCH, N_NA_LAYERS, PAST_LEN, C_HEADS, C_HEAD_DIM), 1.0),
        "c": nrm(9, (DEC_BATCH, D), 1.0),
        "c_ctx": nrm(10, (D,), 1.0),
        "norm_mix": 1.0 + nrm(11, (DEPTH, D), 0.01),
        "norm_ffn": 1.0 + nrm(12, (DEPTH, D), 0.01),
        "norm_final": 1.0 + nrm(13, (D,), 0.01),
        "ada_w": nrm(14, (DEPTH, D, 6 * D), 0.5 * D ** -0.5),
        "ada_b": nrm(15, (DEPTH, 6 * D), 0.01),
        "ab_w_in": nrm(16, (N_AB_LAYERS, D, AB_IN_WIDTH), D ** -0.5),
        "ab_w_out": nrm(17, (N_AB_LAYERS, AB_OUT_WIDTH, D), AB_OUT_WIDTH ** -0.5),
        "ab_q_norm": 1.0 + nrm(18, (N_AB_LAYERS, A_HEAD_DIM), 0.01),
        "ab_k_norm": 1.0 + nrm(19, (N_AB_LAYERS, A_HEAD_DIM), 0.01),
        "ab_gate_bias": jnp.array([0.0, 3.0, 0.0, 3.0], jnp.float32)[None, :, None]
                        + nrm(20, (N_AB_LAYERS, 4, B_HEADS), 0.1),
        "ab_out_norm": 1.0 + nrm(21, (N_AB_LAYERS, B_HEADS, B_HEAD_DIM), 0.01),
        "na_w_in": nrm(22, (N_NA_LAYERS, D, 3 * C_WIDTH), D ** -0.5),
        "na_w_out": nrm(23, (N_NA_LAYERS, C_WIDTH, D), C_WIDTH ** -0.5),
        "na_rpb": nrm(24, (N_NA_LAYERS, C_HEADS, 2 * NA_ROWS_MAX - 1, 2 * NA_COLS - 1), 0.1),
        "moe_wg": nrm(25, (DEPTH, D, N_GROUPS), D ** -0.5),
        "moe_bg": nrm(26, (DEPTH, N_GROUPS), 0.01),
        "moe_we": nrm(27, (DEPTH, D, N_EXPERTS), D ** -0.5),
        "moe_be": nrm(28, (DEPTH, N_EXPERTS), 0.01),
        "moe_w1": nrm(29, (DEPTH, N_EXPERTS, D, D_EXPERT), D ** -0.5),
        "moe_w3": nrm(30, (DEPTH, N_EXPERTS, D, D_EXPERT), D ** -0.5),
        "moe_w2": nrm(31, (DEPTH, N_EXPERTS, D_EXPERT, D), D_EXPERT ** -0.5),
    }

def reference(x_prompt, x_sample, cache_attn_k, cache_attn_v, state_mlstm_C, state_mlstm_n, state_mlstm_m,
              cache_na_k, cache_na_v, c, c_ctx, norm_mix, norm_ffn, norm_final, ada_w, ada_b,
              ab_w_in, ab_w_out, ab_q_norm, ab_k_norm, ab_gate_bias, ab_out_norm,
              na_w_in, na_w_out, na_rpb, moe_wg, moe_bg, moe_we, moe_be, moe_w1, moe_w3, moe_w2):
    cond_ctx = c_ctx[None, :]
    xp, xs = x_prompt, x_sample
    ak_l, av_l, mc_l, mn_l, mm_l, nk_l, nv_l = [], [], [], [], [], [], []
    for l in range(DEPTH):
        j = l // 2
        common = (norm_mix[l], norm_ffn[l], ada_w[l], ada_b[l])
        moe_p = (moe_wg[l], moe_bg[l], moe_we[l], moe_be[l], moe_w1[l], moe_w3[l], moe_w2[l])
        if l % 2 == 0:
            wts = (ab_w_in[j], ab_w_out[j], ab_q_norm[j], ab_k_norm[j], ab_gate_bias[j], ab_out_norm[j])
            xp, st = adaln_layer(xp, cond_ctx, *common, functools.partial(ab_mixer, *wts), moe_p)
            ak_l.append(st[0]); av_l.append(st[1]); mc_l.append(st[2]); mn_l.append(st[3]); mm_l.append(st[4])
            ctx = (cache_attn_k[:, j], cache_attn_v[:, j], state_mlstm_C[:, j], state_mlstm_n[:, j],
                   state_mlstm_m[:, j])
            xs, _ = adaln_layer(xs, c, *common, functools.partial(ab_mixer, *wts, ctx=ctx), moe_p)
        else:
            wts = (na_w_in[j], na_w_out[j], na_rpb[j])
            xp, st = adaln_layer(xp, cond_ctx, *common, functools.partial(na_mixer, *wts), moe_p)
            nk_l.append(st[0]); nv_l.append(st[1])
            ctx = (cache_na_k[:, j], cache_na_v[:, j])
            xs, _ = adaln_layer(xs, c, *common, functools.partial(na_mixer, *wts, ctx=ctx), moe_p)
    y_prompt = rms_norm(xp, norm_final)
    y_sample = rms_norm(xs, norm_final)
    new_attn_k = jnp.stack(ak_l, axis=1)
    new_attn_v = jnp.stack(av_l, axis=1)
    new_mlstm_C = jnp.stack(mc_l, axis=1)
    new_mlstm_n = jnp.stack(mn_l, axis=1)
    new_mlstm_m = jnp.stack(mm_l, axis=1)
    new_na_k = jnp.stack(nk_l, axis=1)
    new_na_v = jnp.stack(nv_l, axis=1)
    return (y_prompt, y_sample, new_attn_k, new_attn_v, new_mlstm_C, new_mlstm_n, new_mlstm_m, new_na_k, new_na_v)


_drawn_inputs = setup_inputs


def setup_inputs(seed=0):
    import zlib

    import numpy as np

    out = dict(_drawn_inputs(seed))
    spreads = {}
    factors = {'cache_attn_k': 4.041,
     'cache_attn_v': 3.708,
     'state_mlstm_C': 5.603,
     'state_mlstm_n': 8.0,
     'state_mlstm_m': 8.0,
     'norm_mix': 3.286,
     'norm_ffn': 4.956,
     'norm_final': 167.337,
     'ab_q_norm': 8.0,
     'ab_k_norm': 5.658,
     'ab_out_norm': 8.0,
     'na_rpb': 64.0,
     'moe_bg': 8.0,
     'moe_be': 7.144,
     'cache_na_k': 8.0,
     'cache_na_v': 8.0}
    for name, (base, spread) in spreads.items():
        noise = np.random.default_rng([zlib.crc32(name.encode()), seed]).standard_normal(out[name].shape)
        drawn = base * np.exp(spread * noise) if base else spread * noise
        out[name] = jnp.asarray(drawn.astype(out[name].dtype))
    for name, factor in factors.items():
        out[name] = (out[name] * factor).astype(out[name].dtype)
    return out
```

```python
from contextlib import ExitStack

import numpy as np

import concourse.bass as bass
from concourse import mybir

P = 128
D = 1024
KT = D // P
SEQ, DEC_SEQ, PAST = 128, 256, 128
NT = (SEQ + DEC_SEQ) // P
TOKENS = NT * P
GRID_W = 64
ROWS = DEC_SEQ // GRID_W
A_HEADS, A_KV, HD = 8, 2, 64
B_HEADS, BD = 4, 128
C_HEADS = 16
NA_ROWS_MAX, NA_COLS = 8, 16
AB_W = A_HEADS * HD + 2 * A_KV * HD + 4 * B_HEADS * BD + 4 * B_HEADS
NA_W = 3 * C_HEADS * HD
AQ, AK, AV = 0, A_HEADS * HD, A_HEADS * HD + A_KV * HD
BQ = AV + A_KV * HD
BK, BV, BO = BQ + B_HEADS * BD, BQ + 2 * B_HEADS * BD, BQ + 3 * B_HEADS * BD
BG = BO + B_HEADS * BD
QK_HEADS = A_HEADS + A_KV
GROUPS, PER_GROUP = 4, 8
EXPERTS = GROUPS * PER_GROUP
FF = 512
BLOCK = 64
OVER = (2 * TOKENS - 1) // BLOCK
SLOTS = (EXPERTS + OVER) * BLOCK
PAIRS = 2 * TOKENS
EPS = 1e-6
FAR = 1.0e30
SKIP = 1.0e5

RING = 6
CHUNK = 4096
ADA_CHUNKS = 6 * D // 512
AB_CHUNKS = (AB_W + 511) // 512
NA_CHUNKS = NA_W // 512
OUT_CHUNKS = D // 512

F32 = mybir.dt.float32
I32 = mybir.dt.int32
U32 = mybir.dt.uint32
ALU = mybir.AluOpType
ACT = mybir.ActivationFunctionType
AX = mybir.AxisListType.X

KEEP = {}
_at = 0
for _name, _n in (("ident", 128), ("trif", 128), ("ones", 128), ("flip", 128), ("window", 64), ("iota", 32),
                  ("first", 32), ("half", 1), ("eps", 1), ("tok", 12)):
    KEEP[_name] = slice(_at, _at + _n)
    _at += _n
NKEEP = _at
EARLY = {}
_at = 0
for _name, _n in (("trib", 128), ("maskf", 128), ("maskb", 128), ("cos", 128), ("sin", 128)):
    EARLY[_name] = slice(_at, _at + _n)
    _at += _n
NEARLY = _at


def tables():
    keep = np.zeros((P, NKEEP), np.float32)
    early = np.zeros((P, NEARLY), np.float32)
    p = np.arange(P)
    keep[:, KEEP["ident"]] = np.eye(P)
    keep[:, KEEP["trif"]] = p[:, None] <= p[None, :]
    keep[:, KEEP["ones"]] = 1.0
    col = p % GRID_W
    mirror = p - col + GRID_W - 1 - col
    keep[p, KEEP["flip"].start + mirror] = 1.0
    c = GRID_W - 1 - col
    start = np.clip(c - NA_COLS // 2, 0, GRID_W - NA_COLS)
    k = np.arange(GRID_W)
    inside = (k[None, :] >= start[:, None]) & (k[None, :] < start[:, None] + NA_COLS)
    keep[:, KEEP["window"]] = np.where(inside, 0.0, -FAR)
    keep[:, KEEP["iota"]] = np.arange(32)
    keep[:, KEEP["first"]] = np.arange(32) * BLOCK
    keep[:, KEEP["half"]] = (p >= BLOCK)[:, None]
    keep[:, KEEP["eps"]] = EPS
    t, k2 = np.meshgrid(np.arange(NT), np.arange(2), indexing="ij")
    token = t[None] * P + p[:, None, None]
    pair = 2 * token + k2[None]
    keep[:, KEEP["tok"]] = np.stack([2 * token + 0 * pair, 2 * pair], -1).reshape(P, 12)
    early[:, EARLY["trib"]] = p[:, None] >= p[None, :]
    early[:, EARLY["maskf"]] = np.where(p[:, None] >= p[None, :], 0.0, -FAR)
    early[:, EARLY["maskb"]] = np.where(p[:, None] <= p[None, :], 0.0, -FAR)
    half = HD // 2
    freqs = 1.0 / (10000.0 ** (np.arange(0, half, 2, dtype=np.float32) / half))
    tok = np.arange(DEC_SEQ)
    rot = []
    for pos in (tok // GRID_W, tok % GRID_W):
        rot.append(pos[:, None].astype(np.float32) * freqs[None, :])
    cos = np.concatenate([np.cos(rot[0]), np.cos(rot[0]), np.cos(rot[1]), np.cos(rot[1])], -1)
    sin = np.concatenate([-np.sin(rot[0]), np.sin(rot[0]), -np.sin(rot[1]), np.sin(rot[1])], -1)
    early[:, EARLY["cos"]] = cos.reshape(2, P, HD).transpose(1, 0, 2).reshape(P, 2 * HD)
    early[:, EARLY["sin"]] = sin.reshape(2, P, HD).transpose(1, 0, 2).reshape(P, 2 * HD)
    return keep, early


def build(nc, a, o):
    ctx = ExitStack()
    with ctx:
        def sb(name, shape, dt=F32):
            return ctx.enter_context(nc.sbuf_tensor(name, shape, dt))

        def sem(name):
            return ctx.enter_context(nc.semaphore(name))

        ring = sb("ring", [P, RING, CHUNK])
        x = sb("x", [P, NT, D])
        area_h = sb("area_h", [P, 3 * D])
        area_t = sb("area_t", [P, 3 * D])
        area_q = sb("area_q", [P, NT * NA_W])
        area_m = sb("area_m", [P, 6144])
        area_g = sb("area_g", [P, 2 * D])
        keep = sb("keep", [P, NKEEP])
        wge = sb("wge", [P, KT, GROUPS + EXPERTS])
        ctx_kv = sb("ctx_kv", [P, 2, A_KV * HD])
        condr = sb("condr", [P, 2, KT])
        cond32 = sb("cond32", [P, KT, 32])
        small = sb("small", [P, 432])
        used = [0]

        def cut(*shape):
            n = int(np.prod(shape))
            v = small[:, used[0]:used[0] + n]
            used[0] += n
            if len(shape) == 2:
                v = v.rearrange("p (a b) -> p a b", a=shape[0])
            if len(shape) == 3:
                v = v.rearrange("p (a b c) -> p a b c", a=shape[0], b=shape[1])
            return v

        banks = [ctx.enter_context(nc.psum_tensor(f"bank{i}", [P, 512], F32)) for i in range(8)]
        mod_dram = nc.dram_tensor("mod_raw", [2, 2, 6 * D], F32).ap()
        modf_dram = nc.dram_tensor("mod_ready", [2, 6, 2, D], F32).ap()
        h2_dram = [nc.dram_tensor(f"h2_rows{l}", [2 * TOKENS, D // 2], F32).ap() for l in range(2)]
        pair_dram = [nc.dram_tensor(f"pair_rows{l}", [2 * PAIRS, D // 2], F32).ap() for l in range(2)]
        slot_dram = [nc.dram_tensor(f"slot_rows{l}", [SLOTS, 2], F32).ap() for l in range(2)]

        ident, trif, ones, flip = (keep[:, KEEP[n]] for n in ("ident", "trif", "ones", "flip"))
        h = area_h[:, :].rearrange("p (t d) -> p t d", t=NT)
        hT = area_t[:, :].rearrange("p (k n) -> p k n", k=KT)
        qkv = [area_q[:, 0:NT * AB_W].rearrange("p (t n) -> p t n", t=NT),
               area_q[:, :].rearrange("p (t n) -> p t n", t=NT)]
        early = area_q[:, NT * AB_W:NT * AB_W + NEARLY]
        modA = area_m[:, 0:2 * D].rearrange("p (c d) -> p c d", c=2)
        modB = area_m[:, 2 * D:4 * D].rearrange("p (c d) -> p c d", c=2)
        modG = area_g[:, :].rearrange("p (c d) -> p c d", c=2)
        modsb = area_m[:, 5120:6144].rearrange("p (b c n) -> p b c n", b=2, c=4)
        cmod = area_m[:, 4096:4096 + 96].rearrange("p (c v i) -> p c v i", c=2, v=6)
        cada = area_m[:, 4192:4192 + 48].rearrange("p (v i) -> p v i", v=6)
        cgain = area_m[:, 4240:4240 + 16].rearrange("p (v i) -> p v i", v=2)
        hm = area_h[:, 0:NT * 512].rearrange("p (t n) -> p t n", t=NT)
        wexp = area_h[:, 1536:2560].rearrange("p (u s) -> p u s", u=8)
        amat = area_h[:, 2560:3072].rearrange("p (u s) -> p u s", u=4)
        bqT = area_t[:, 0:1536].rearrange("p (h n) -> p h n", h=4)
        bkT = area_t[:, 1536:3072].rearrange("p (h n) -> p h n", h=4)
        diag = area_m[:, 0:1024].rearrange("p (u s) -> p u s", u=8)
        amatT = area_m[:, 1024:1536].rearrange("p (u s) -> p u s", u=4)
        tmp1 = area_m[:, 1536:2048].rearrange("p (u s) -> p u s", u=4)
        kw = area_m[:, 2048:2560].rearrange("p (u s) -> p u s", u=4)
        Cst = area_m[:, 2560:3584].rearrange("p (u s) -> p u s", u=8)
        qkgain = area_m[:, 3584:4224].rearrange("p (u s) -> p u s", u=QK_HEADS)
        ogain = area_m[:, 4224:4736].rearrange("p (u s) -> p u s", u=4)
        gbias = area_m[:, 4736:4752]
        Cout = area_g[:, 0:1024].rearrange("p (u s) -> p u s", u=8)
        kdup = area_m[:, 0:1024].rearrange("p (v s x c) -> p v s x c", v=A_KV, s=4, x=2)
        prob = area_g[:, 0:768].rearrange("p (b n) -> p b n", b=2)
        probT = area_g[:, 768:1536].rearrange("p (b n) -> p b n", b=2)
        qT = area_h[:, 0:768].rearrange("p (b n) -> p b n", b=2)
        kT = area_h[:, 768:1792].rearrange("p (b n) -> p b n", b=2)
        na_ctx = area_t[:, 0:2 * D].rearrange("p (v n) -> p v n", v=2)
        bias_na = area_m[:, :].rearrange("p (h r c) -> p h r c", h=C_HEADS, r=6)
        mixed = area_m[:, 4608:5632].rearrange("p (b n) -> p b n", b=2)
        xg = [area_t[:, 512 * i:512 * i + 512] for i in range(2)]
        xT = [area_t[:, 1024 + 512 * i:1536 + 512 * i].rearrange("p (k s) -> p k s", k=4) for i in range(2)]
        hidT = [area_t[:, 2048 + 256 * i:2304 + 256 * i].rearrange("p (k s) -> p k s", k=4) for i in range(2)]
        upT = [area_t[:, 2560 + 256 * i:2816 + 256 * i].rearrange("p (k s) -> p k s", k=4) for i in range(2)]
        hs = [area_q[:, 512 * i:512 * i + 512] for i in range(2)]
        ysb = [area_q[:, 1024 + 512 * i:1536 + 512 * i] for i in range(2)]
        rt = area_q[:, 2048:3072]
        slots_f = area_q[:, 3072:3072 + 2 * (EXPERTS + OVER)].rearrange("p (e v) -> p e v", v=2)
        slots_i = area_q[:, 3200:3200 + 2 * (EXPERTS + OVER)].bitcast(U32).rearrange("p (e v) -> p e v", v=2)
        pairs = area_q[:, 3072:9216].rearrange("p (t k d) -> p t k d", t=NT, k=2)

        ss, rstd = cut(4), cut(4)
        qss, qrs = cut(NT, QK_HEADS), cut(NT, QK_HEADS)
        gates, absf = cut(NT, 16), cut(NT, 8)
        li, lf = cut(3, 8), cut(3, 8)
        bcum, btot, rrow = cut(3, 8), cut(3, 8), cut(3, 8)
        mstate, gcol, gall, gpick = cut(8), cut(8), cut(8), cut(8)
        expo = cut(4, 8)
        den, dena, nst, nout, mout = cut(4), cut(4), cut(8), cut(8), cut(8)
        negm, lsum, rlsum = cut(4), cut(4), cut(4)
        wtop = cut(NT, 2)
        hss = cut(NT, 4)
        assert used[0] <= 432, used
        eid_i = sb("eid_i", [P, OVER + 1], I32)
        slot_u = sb("slot_u", [P, 2, NT], U32)
        m0_sb = sb("m0_sb", [P, 8])
        rbias_sb = sb("rbias_sb", [P, GROUPS + EXPERTS])

        landed = [sem(f"weights_landed{i}") for i in range(RING)]
        S = {n: sem(n) for n in (
            "x_loaded", "keep_loaded", "early_loaded", "cond_loaded", "cond_silu", "cond_rep",
            "ada_done", "ada_copied", "ada_stored0", "ada_stored1", "cmod_loaded", "cmod_ready", "cmod_stored",
            "modAB_loaded", "modG_loaded", "squares", "h_ready", "trans_done", "trans_copied",
            "proj_done", "proj_copied_dve", "proj_copied_act", "small_loaded", "wge_loaded",
            "dve_step", "act_step", "qk_ready", "kv_stored", "gates_in", "gates_exp", "gates_log", "lf_ready",
            "cum_done", "bt_done", "bt_copied_q", "bt_copied_k", "diag_ready", "rows_done", "expo_ready", "expo_done",
            "wexp_ready", "wexp_done", "bs_done", "amat_ready", "amatT_done", "amatT_copied", "bnum_done",
            "kw_ready", "bupd_done", "combined", "cstate_ready", "state_loaded", "state_stored", "hm_squares", "hm_rooted", "qk_squares", "qk_rooted",
            "ogate_done", "bout_ready", "kdup_ready", "na_ctx_loaded", "bias_loaded", "bias_ready",
            "pair_done", "qT_copied", "kT_copied", "scores_done", "max_ready", "prob_ready", "probT_done",
            "probT_copied", "pv_done", "heads_out", "outT_done", "outT_copied", "out_done", "x_mixed",
            "h2_stored", "logits_done", "route_exp", "route_exped", "chosen", "ranks_done", "slots_ready",
            "table_cleared", "slots_scattered", "slots_loaded", "index_ready", "xg_cleared", "over_ready",
            "pairs_loaded0", "pairs_loaded1", "pairs_loaded2", "pair_scaled", "x_moe",
            "y_ready", "y_stored", "gfin_loaded", "table_filled", "x_rest", "ctx_v", "wge_w")}

        def block_sems(tag):
            return {n: sem(f"{tag}_{n}") for n in (
                "gathered0", "gathered1", "xT_done", "xT_copied", "hid_done", "silu_done", "up_copied", "hidT_done",
                "upT_copied", "hidT_ready", "y_done", "y_copied", "scattered0", "scattered1")}

        M = block_sems("moe")
        V = block_sems("over")
        over_landed = [sem(f"over_landed{i}") for i in range(3)]

        START = {}
        n = 0
        for key, cnt in ((("ada", 0), ADA_CHUNKS), (("in", 0), AB_CHUNKS), (("ada", 1), ADA_CHUNKS),
                         (("out", 0), OUT_CHUNKS), (("moe", 0), 3 * EXPERTS), (("in", 1), NA_CHUNKS),
                         (("out", 1), OUT_CHUNKS), (("moe", 1), 3 * EXPERTS)):
            START[key] = n
            n += cnt
        IN_CHUNKS = (AB_CHUNKS, NA_CHUNKS)
        IN_W = (AB_W, NA_W)
        PROJ0 = (0, AB_CHUNKS * NT)

        def place(n):
            return n % RING

        def when(n):
            return 16 * (n // RING + 1)

        def freed(eng, n):
            for key in START:
                kind, l = key
                cnt = {"ada": ADA_CHUNKS, "in": IN_CHUNKS[l], "out": OUT_CHUNKS, "moe": 3 * EXPERTS}[kind]
                c = n - START[key]
                if not 0 <= c < cnt:
                    continue
                if kind == "ada":
                    eng.wait_ge(S["ada_done"], l * ADA_CHUNKS + c + 1)
                if kind == "in":
                    eng.wait_ge(S["proj_done"], PROJ0[l] + NT * (c + 1))
                if kind == "out":
                    eng.wait_ge(S["out_done"], l * NT * OUT_CHUNKS + NT * OUT_CHUNKS)
                if kind == "moe":
                    e, j = divmod(c, 3)
                    eng.wait_ge(M["y_done"] if j == 2 else M["hid_done"], l * EXPERTS + e + 1)

        def wchunk(n, k):
            return ring[:, place(n), :].rearrange("p (k n) -> p k n", k=k)

        def expert_dram(l, e, j):
            one = (l, e) if isinstance(e, int) else (l, bass.ds(e, 1))
            if j == 2:
                v = a["moe_w2"][l].rearrange("e (p k) n -> e p (k n)", k=4)
                return v[e] if isinstance(e, int) else v[bass.ds(e, 1)].rearrange("e p n -> (e p) n")
            w = a["moe_w1" if j == 0 else "moe_w3"][l].rearrange("e (h p k) n -> e p h (k n)", h=2, k=4)
            return w[e] if isinstance(e, int) else w[bass.ds(e, 1)].rearrange("e p h n -> (e p) h n")

        def expert_dst(view, j):
            return view if j == 2 else view.rearrange("p (h n) -> p h n", h=2)

        STAGES = ((0, 0), (1, 2), (2, 1))
        NP = (A_HEADS // 2, C_HEADS // 2)
        NU = tuple(n * NT * 2 for n in NP)
        U0 = (0, NU[0])

        def unit(l, i):
            return i // (2 * NT), i // 2 % NT, i % 2

        def keys_of(t):
            return (0, P) if t == 0 else (P, 4 * P)

        def gath(e, u, base):
            if isinstance(e, int):
                return 16 * ((e + base) // 2 + 1)
            return e * 8 + (8 * base - 8 * u + 16)

        block = ctx.enter_context(nc.Block())

        @block.sync
        def _(sp):
            def load(n, dst, src):
                if n >= RING:
                    freed(sp, n - RING)
                sp.dma_start(dst, src).then_inc(landed[place(n)], 16)

            def load_rows(key, w_dram, width, how):
                v = w_dram.rearrange(how, p=P)
                for c in range((width + 511) // 512):
                    n = START[key] + c
                    w = min(512, width - 512 * c)
                    load(n, wchunk(n, KT)[:, :, 0:w], v[:, :, 512 * c:512 * c + w])

            def load_experts(l):
                base = START["moe", l]
                prev = base - RING

                def one(e, u):
                    for j in range(3):
                        at = place(base + 3 * u + j)
                        dst = expert_dst(ring[:, at, :], j)
                        if isinstance(e, int) and e < 2:
                            freed(sp, base + 3 * e + j - RING)
                        else:
                            sp.wait_ge(M["y_done"] if j == 2 else M["hid_done"], e + (l * EXPERTS - 1))
                        sp.dma_start(dst, expert_dram(l, e, j)).then_inc(landed[at], 16)

                one(0, 0)
                one(1, 1)
                with sp.Fori(1, EXPERTS // 2) as i:
                    for u in range(2):
                        one(sp.snap(i * 2 + u), u)

            def load_overflow(l):
                sp.wait_ge(S["over_ready"], l + 1)
                n_over = sp.value_load(eid_i[0:1, OVER:OVER + 1], min_val=0, max_val=OVER)
                with sp.If(n_over > 0):
                    sp.wait_ge(M["y_done"], (l + 1) * EXPERTS)

                    def one(b, first):
                        e = sp.value_load(eid_i[0:1, 0:1] if first else eid_i[0:1, bass.ds(b, 1)],
                                          min_val=0, max_val=EXPERTS - 1)
                        for j in range(3):
                            if not first:
                                sp.wait_ge(V["y_done"] if j == 2 else V["hid_done"], b + l * OVER)
                            sp.dma_start(expert_dst(ring[:, j, :], j), expert_dram(l, e, j)).then_inc(over_landed[j], 16)

                    one(0, True)
                    with sp.Fori(1, OVER) as b:
                        one(b, False)
                    sp.wait_ge(V["y_done"], (l + 1) * OVER)

            load_rows(("ada", 0), a["ada_w"][0], 6 * D, "(p k) n -> p k n")
            load_rows(("in", 0), a["ab_w_in"][0], AB_W, "(k p) n -> p k n")
            load_rows(("ada", 1), a["ada_w"][1], 6 * D, "(p k) n -> p k n")
            load_rows(("out", 0), a["ab_w_out"][0], D, "(k p) n -> p k n")
            load_experts(0)
            load_overflow(0)
            load_rows(("in", 1), a["na_w_in"][0], NA_W, "(k p) n -> p k n")
            load_rows(("out", 1), a["na_w_out"][0], D, "(k p) n -> p k n")
            load_experts(1)
            load_overflow(1)

        @block.tensor
        def _(pe):
            def ada(l, c):
                n = START["ada", l] + c
                if l == 0 and c == 0:
                    pe.wait_ge(S["cond_rep"], 1)
                pe.wait_ge(landed[place(n)], when(n))
                g = l * 3 + c // 4
                if c % 4 == 0 and g:
                    pe.wait_ge(S["ada_copied"], g)
                w = wchunk(n, KT)
                for k in range(KT):
                    for j in range(4):
                        mm = pe.matmul(banks[7][32 * j:32 * j + 32, 128 * (c % 4):128 * (c % 4) + 128],
                                       cond32[:, k, :], w[:, k, 128 * j:128 * j + 128],
                                       start=(k == 0), stop=(k == KT - 1), skip_group_check=True)
                mm.then_inc(S["ada_done"], 1)

            def transpose_rows(idx):
                for t in range(NT):
                    pe.wait_ge(S["h_ready"], NT * idx + t + 1)
                    for half in range(2):
                        n = 2 * (NT * idx + t) + half
                        if n >= 2:
                            pe.wait_ge(S["trans_copied"], n - 1)
                        for k in range(4):
                            d0 = (4 * half + k) * P
                            mm = pe.transpose(banks[n % 2][:, k * P:k * P + P], h[:, t, d0:d0 + P], ident)
                        mm.then_inc(S["trans_done"], 1)

            def project(l):
                for c in range(IN_CHUNKS[l]):
                    n = START["in", l] + c
                    w = min(512, IN_W[l] - 512 * c)
                    pe.wait_ge(landed[place(n)], when(n))
                    for t in range(NT):
                        g = PROJ0[l] + NT * c + t
                        if c == 0:
                            pe.wait_ge(S["trans_copied"], 2 * (NT * 2 * l + t + 1))
                        if g >= 4:
                            pe.wait_ge(S["proj_copied_act" if g % 2 else "proj_copied_dve"], (g - 4) // 2 + 1)
                        for k in range(KT):
                            mm = pe.matmul(banks[2 + g % 4][:, 0:w], hT[:, k, t * P:t * P + P],
                                           wchunk(n, KT)[:, k, 0:w], start=(k == 0), stop=(k == KT - 1))
                        mm.then_inc(S["proj_done"], 1)

            def mlstm():
                for n in range(2 * NT):
                    t, side = n // 2, n % 2
                    if n == 0:
                        pe.wait_ge(S["proj_copied_dve"], AB_CHUNKS * NT // 2)
                        pe.wait_ge(S["proj_copied_act"], AB_CHUNKS * NT // 2)
                    if n >= 2:
                        pe.wait_ge(S["bt_copied_k" if side else "bt_copied_q"], t)
                    for hh in range(B_HEADS):
                        c0 = (BK if side else BQ) + hh * BD
                        mm = pe.transpose(banks[3 + side][:, hh * P:hh * P + P], qkv[0][:, t, c0:c0 + BD], ident)
                    mm.then_inc(S["bt_done"], 1)
                pe.wait_ge(S["lf_ready"], 1)
                pe.wait_ge(S["early_loaded"], 16)
                for s in range(3):
                    pe.matmul(banks[0][:, 16 * s:16 * s + 4], trif, lf[:, s, 0:4], start=True, stop=True)
                    pe.matmul(banks[0][:, 16 * s + 4:16 * s + 8], early[:, EARLY["trib"]], lf[:, s, 4:8],
                              start=True, stop=True)
                    mm = pe.matmul(banks[0][:, 16 * s + 8:16 * s + 16], ones, lf[:, s, :], start=True, stop=True)
                mm.then_inc(S["cum_done"], 1)
                for s in range(3):
                    pe.wait_ge(S["diag_ready"], s + 1)
                    for d in range(2):
                        mm = pe.matmul(banks[1 + d][:, :], ones, diag[:, 4 * d:4 * d + 4, :], start=True, stop=True)
                    mm.then_inc(S["rows_done"], 1)
                    for d in range(2):
                        t = STAGES[s][d]
                        tok = slice(t * P, t * P + P)
                        v = 2 * s + d
                        if v == 0:
                            pe.wait_ge(S["bt_copied_q"], NT)
                            pe.wait_ge(S["bt_copied_k"], NT)
                        else:
                            pe.wait_ge(S["amat_ready"], v)
                        for hh in range(B_HEADS):
                            mm = pe.matmul(banks[3][:, hh * P:hh * P + P], bqT[:, hh, tok], bkT[:, hh, tok],
                                           start=True, stop=True)
                        mm.then_inc(S["bs_done"], 1)
                        pe.wait_ge(S["amat_ready"], v + 1)
                        for hh in range(B_HEADS):
                            mm = pe.transpose(banks[4][:, hh * P:hh * P + P], amat[:, hh, :], ident)
                        mm.then_inc(S["amatT_done"], 1)
                        if s == 1:
                            pe.wait_ge(S["state_loaded"], 48)
                        if s == 2:
                            pe.wait_ge(S["cstate_ready"], 4)
                        if v > 0:
                            pe.wait_ge(S["combined"], v)
                        if s > 0:
                            for hh in range(B_HEADS):
                                pe.matmul(banks[6][:, hh * P:hh * P + P], bqT[:, hh, tok], Cst[:, 4 * d + hh, :],
                                          start=True, stop=True)
                            pe.wait_ge(S["expo_ready"], s + 1)
                            for hh in range(B_HEADS):
                                pe.matmul(banks[1][:, 8 * d + hh:8 * d + hh + 1], bqT[:, hh, tok],
                                          nst[:, 4 * d + hh:4 * d + hh + 1], start=True, stop=True)
                        pe.wait_ge(S["amatT_copied"], v + 1)
                        for hh in range(B_HEADS):
                            mm = pe.matmul(banks[5][:, hh * P:hh * P + P], amatT[:, hh, :],
                                           qkv[0][:, t, BV + hh * BD:BV + hh * BD + BD], start=True, stop=True)
                        mm.then_inc(S["bnum_done"], 1)
                        if s < 2:
                            pe.wait_ge(S["kw_ready"], v + 1)
                            if v > 0:
                                pe.wait_ge(S["cstate_ready"], v)
                            for hh in range(B_HEADS):
                                pe.matmul(banks[0][:, hh * P:hh * P + P], kw[:, hh, :],
                                          qkv[0][:, t, BV + hh * BD:BV + hh * BD + BD], start=True, stop=True)
                            for hh in range(B_HEADS):
                                mm = pe.matmul(banks[2][:, hh:hh + 1], kw[:, hh, :], ones[:, 0:1],
                                               start=True, stop=True)
                            mm.then_inc(S["bupd_done"], 1)

            def turn_queries(l, j):
                if l == 0 and j == 0:
                    pe.wait_ge(S["kdup_ready"], 1)
                    pe.wait_ge(S["ctx_v"], 16)
                if l == 1 and j == 0:
                    for name in ("proj_copied_dve", "proj_copied_act"):
                        pe.wait_ge(S[name], (PROJ0[1] + NA_CHUNKS * NT) // 2)
                    pe.wait_ge(S["na_ctx_loaded"], 32)
                    pe.wait_ge(S["bias_ready"], 1)
                g = (0, NP[0])[l] + j
                if g:
                    pe.wait_ge(S["kT_copied"], g)
                for t in range(NT):
                    mm = pe.transpose(banks[5][:, t * P:t * P + P], qkv[l][:, t, 2 * HD * j:2 * HD * j + 2 * HD], ident)
                mm.then_inc(S["pair_done"], 1)

            def turn_keys(l, j):
                g = (0, NP[0])[l] + j
                pe.wait_ge(S["qT_copied"], g + 1)
                for s in range(4):
                    if l == 0:
                        src = kdup[:, j // 2, s, :, :]
                    elif s == 1:
                        src = na_ctx[:, 0, 2 * HD * j:2 * HD * j + 2 * HD]
                    else:
                        src = qkv[1][:, (0, None, 1, 2)[s], D + 2 * HD * j:D + 2 * HD * j + 2 * HD]
                    mm = pe.transpose(banks[5][:, s * P:s * P + P], src, ident)
                mm.then_inc(S["pair_done"], 1)

            def scores(l, i):
                j, t, hh = unit(l, i)
                U = U0[l] + i
                k0, k1 = keys_of(t)
                g = (0, NP[0])[l] + j
                pe.wait_ge(S["qT_copied"], g + 1)
                pe.wait_ge(S["kT_copied"], g + 1)
                if U >= 2:
                    pe.wait_ge(S["prob_ready"], U - 1)
                rows = slice(64 * hh, 64 * hh + 64)
                bank = banks[U % 2]
                biased = l == 1 and t > 0
                mm = pe.matmul(bank[:, 0:k1 - k0], qT[rows, g % 2, t * P:t * P + P], kT[rows, g % 2, k0:k1],
                               start=True, stop=not biased)
                if biased:
                    r0 = 4 - 2 * t
                    mm = pe.matmul(bank[:, P:3 * P], flip, bias_na[:, 2 * j + hh, r0:r0 + ROWS, :],
                                   start=False, stop=True)
                mm.then_inc(S["scores_done"], 1)

            def turn_probs(l, i):
                j, t, hh = unit(l, i)
                U = U0[l] + i
                pe.wait_ge(S["prob_ready"], U + 1)
                if U >= 2:
                    pe.wait_ge(S["probT_copied"], U - 1)
                k0, k1 = keys_of(t)
                for s in range((k1 - k0) // P):
                    mm = pe.transpose(banks[2 + U % 2][:, s * P:s * P + P], prob[:, U % 2, s * P:s * P + P], ident)
                mm.then_inc(S["probT_done"], 1)

            def values(l, i):
                j, t, hh = unit(l, i)
                U = U0[l] + i
                pe.wait_ge(S["probT_copied"], U + 1)
                if U >= 2:
                    pe.wait_ge(S["heads_out"], U - 1)
                c0 = (AV + (j // 2) * HD) if l == 0 else 2 * D + (2 * j + hh) * HD
                vs = [qkv[l][:, tt, c0:c0 + HD] for tt in range(NT)]
                if l == 0:
                    cached = ctx_kv[:, 1, (j // 2) * HD:(j // 2) * HD + HD]
                else:
                    cached = na_ctx[:, 1, (2 * j + hh) * HD:(2 * j + hh) * HD + HD]
                vs = vs[0:1] if t == 0 else [cached] + vs[1:]
                for s, v in enumerate(vs):
                    mm = pe.matmul(banks[4 + 2 * (U % 2)][:, 0:HD], probT[:, U % 2, s * P:s * P + P], v,
                                   start=(s == 0), stop=(s == len(vs) - 1))
                mm.then_inc(S["pv_done"], 1)

            def attention(l):
                turn_queries(l, 0)
                turn_keys(l, 0)
                for i in range(NU[l] + 2):
                    if i % 6 == 2 and i // 6 + 1 < NP[l]:
                        turn_queries(l, i // 6 + 1)
                    if i % 6 == 4 and i // 6 + 1 < NP[l]:
                        turn_keys(l, i // 6 + 1)
                    if i < NU[l]:
                        scores(l, i)
                    if 1 <= i <= NU[l]:
                        turn_probs(l, i - 1)
                    if i >= 2:
                        values(l, i - 2)
                    if l == 0 and i % 2 == 1 and i // 2 < ADA_CHUNKS:
                        ada(1, i // 2)

            def project_out(l):
                for t in range(NT):
                    for half in range(2):
                        n = 2 * (NT * l + t) + half
                        if n % (2 * NT) == 0:
                            pe.wait_ge(S["heads_out"], U0[l] + NU[l])
                            if l == 0:
                                pe.wait_ge(S["bout_ready"], NT)
                        if n >= 2:
                            pe.wait_ge(S["outT_copied"], n - 1)
                        c0 = BQ if (l == 0 and half == 1) else 512 * half
                        for k in range(4):
                            mm = pe.transpose(banks[n % 2][:, k * P:k * P + P],
                                              qkv[l][:, t, c0 + k * P:c0 + k * P + P], ident)
                        mm.then_inc(S["outT_done"], 1)
                for t in range(NT):
                    pe.wait_ge(S["outT_copied"], 2 * (NT * l + t + 1))
                    for c in range(OUT_CHUNKS):
                        n = START["out", l] + c
                        pe.wait_ge(landed[place(n)], when(n))
                        g = l * NT * OUT_CHUNKS + t * OUT_CHUNKS + c
                        if g >= 2:
                            pe.wait_ge(S["x_mixed"], g - 1)
                        for k in range(KT):
                            mm = pe.matmul(banks[2 + g % 2][:, :], hT[:, k, t * P:t * P + P],
                                           wchunk(n, KT)[:, k, :], start=(k == 0), stop=(k == KT - 1))
                        mm.then_inc(S["out_done"], 1)

            def route(l):
                pe.wait_ge(S["wge_w"], 32 * (l + 1))
                for t in range(NT):
                    pe.wait_ge(S["trans_copied"], 2 * (NT * (2 * l + 1) + t + 1))
                    for k in range(KT):
                        mm = pe.matmul(banks[6][:, 36 * t:36 * t + 36], hT[:, k, t * P:t * P + P], wge[:, k, :],
                                       start=(k == 0), stop=(k == KT - 1))
                mm.then_inc(S["logits_done"], 1)
                pe.wait_ge(S["chosen"], l + 1)
                chosen = rt[:, 0:96].rearrange("p (t e) -> p t e", t=NT)
                for t in range(NT + 1):
                    for s in range(min(t, NT - 1) + 1 if t < NT else NT):
                        mm = pe.matmul(banks[0][:, 32 * t:32 * t + 32], trif if s == t else ones, chosen[:, s, :],
                                       start=(s == 0), stop=(s == (t if t < NT else NT - 1)))
                mm.then_inc(S["ranks_done"], 1)

            def turn_tokens(Q, e, u, base):
                pe.wait_ge(Q[f"gathered{u}"], gath(e, u, base))
                if not (isinstance(e, int) and e + base < 2):
                    pe.wait_ge(Q["xT_copied"], e + (base - 1))
                for k in range(4):
                    mm = pe.transpose(banks[u][:, k * P:k * P + P], xg[u][:, k:512:4], ident)
                mm.then_inc(Q["xT_done"], 1)

            def hidden(Q, e, u, base, w1, w3):
                pe.wait_ge(Q["xT_copied"], e + (base + 1))
                if not (isinstance(e, int) and e + base < 2):
                    pe.wait_ge(Q["silu_done"], e + (base - 1))
                    pe.wait_ge(Q["up_copied"], e + (base - 1))
                for k in range(KT):
                    lhsT = xT[u][:, k % 4, 64 * (k // 4):64 * (k // 4) + 64]
                    pe.matmul(banks[2 + u][0:64, :], lhsT, w1[:, k, :], start=(k == 0), stop=(k == KT - 1))
                    mm = pe.matmul(banks[2 + u][64:128, :], lhsT, w3[:, k, :], start=(k == 0), stop=(k == KT - 1))
                mm.then_inc(Q["hid_done"], 1)

            def turn_hidden(Q, e, u, base):
                pe.wait_ge(Q["silu_done"], e + (base + 1))
                pe.wait_ge(Q["up_copied"], e + (base + 1))
                if not (isinstance(e, int) and e + base < 2):
                    pe.wait_ge(Q["hidT_ready"], e + (base - 1))
                for k in range(4):
                    mm = pe.transpose(banks[4 + u][:, k * P:k * P + P], hs[u][:, k:512:4], ident)
                mm.then_inc(Q["hidT_done"], 1)

            def down(Q, e, u, base, w2):
                pe.wait_ge(Q["hidT_ready"], e + (base + 1))
                if not (isinstance(e, int) and e + base < 2):
                    pe.wait_ge(Q["y_copied"], e + (base - 1))
                for k in range(4):
                    for j in range(2):
                        mm = pe.matmul(banks[6 + u][64 * j:64 * j + 64, :], hidT[u][:, k, :],
                                       w2[:, k, 512 * j:512 * j + 512], start=(k == 0), stop=(k == 3))
                mm.then_inc(Q["y_done"], 1)

            def experts(l):
                start = START["moe", l]
                base = l * EXPERTS

                def wait_chunk(e, u, j):
                    n = start + 3 * u + j
                    rounds = (e - u) * 8 if isinstance(e, int) else (e * 8 - 8 * u)
                    pe.wait_ge(landed[place(n)], rounds + when(n))

                def one(e, u, last):
                    ws = [wchunk(start + 3 * u + j, 4 if j == 2 else KT) for j in range(3)]
                    wait_chunk(e, u, 0)
                    wait_chunk(e, u, 1)
                    hidden(M, e, u, base, ws[0], ws[1])
                    if not last:
                        turn_tokens(M, e + 1, 1 - u, base)
                    turn_hidden(M, e, u, base)
                    wait_chunk(e, u, 2)
                    down(M, e, u, base, ws[2])

                turn_tokens(M, 0, 0, base)
                one(0, 0, False)
                one(1, 1, False)
                with pe.Fori(1, EXPERTS // 2 - 1) as i:
                    for u in range(2):
                        one(pe.snap(i * 2 + u), u, False)
                one(EXPERTS - 2, 0, False)
                one(EXPERTS - 1, 1, True)

            def overflow(l):
                base = l * OVER
                pe.wait_ge(S["over_ready"], l + 1)
                n_over = pe.value_load(eid_i[0:1, OVER:OVER + 1], min_val=0, max_val=OVER)
                with pe.If(n_over > 0):
                    with pe.Fori(0, OVER) as b:
                        turn_tokens_over(b, base)
                        for j in range(2):
                            pe.wait_ge(over_landed[j], b * 16 + 16 * (base + 1))
                        hidden_over(b, base)
                        turn_hidden_over(b, base)
                        pe.wait_ge(over_landed[2], b * 16 + 16 * (base + 1))
                        down_over(b, base)

            def turn_tokens_over(b, base):
                pe.wait_ge(V["gathered0"], b * 16 + 16 * (base + 1))
                for k in range(4):
                    mm = pe.transpose(banks[0][:, k * P:k * P + P], xg[0][:, k:512:4], ident)
                mm.then_inc(V["xT_done"], 1)

            def hidden_over(b, base):
                pe.wait_ge(V["xT_copied"], b + (base + 1))
                w1 = ring[:, 0, :].rearrange("p (k n) -> p k n", k=KT)
                w3 = ring[:, 1, :].rearrange("p (k n) -> p k n", k=KT)
                for k in range(KT):
                    lhsT = xT[0][:, k % 4, 64 * (k // 4):64 * (k // 4) + 64]
                    pe.matmul(banks[2][0:64, :], lhsT, w1[:, k, :], start=(k == 0), stop=(k == KT - 1))
                    mm = pe.matmul(banks[2][64:128, :], lhsT, w3[:, k, :], start=(k == 0), stop=(k == KT - 1))
                mm.then_inc(V["hid_done"], 1)

            def turn_hidden_over(b, base):
                pe.wait_ge(V["silu_done"], b + (base + 1))
                pe.wait_ge(V["up_copied"], b + (base + 1))
                for k in range(4):
                    mm = pe.transpose(banks[4][:, k * P:k * P + P], hs[0][:, k:512:4], ident)
                mm.then_inc(V["hidT_done"], 1)

            def down_over(b, base):
                pe.wait_ge(V["hidT_ready"], b + (base + 1))
                w2 = ring[:, 2, :].rearrange("p (k n) -> p k n", k=4)
                for k in range(4):
                    for j in range(2):
                        mm = pe.matmul(banks[6][64 * j:64 * j + 64, :], hidT[0][:, k, :],
                                       w2[:, k, 512 * j:512 * j + 512], start=(k == 0), stop=(k == 3))
                mm.then_inc(V["y_done"], 1)

            pe.wait_ge(S["keep_loaded"], 16)
            for c in range(ADA_CHUNKS):
                ada(0, c)
            for l in range(2):
                transpose_rows(2 * l)
                project(l)
                if l == 0:
                    mlstm()
                attention(l)
                project_out(l)
                transpose_rows(2 * l + 1)
                route(l)
                experts(l)
                overflow(l)

        @block.scalar
        def _(act):
            count = {}

            def step(ins, name, hold=False):
                ins.then_inc(S[name], 1)
                count[name] = count.get(name, 0) + 1
                if hold:
                    act.wait_ge(S[name], count[name])

            act.wait_ge(S["cond_loaded"], 32)
            step(act.activation(condr[:, :, :], condr[:, :, :], ACT.Silu), "cond_silu")

            def ada_copy(g):
                act.wait_ge(S["ada_done"], 4 * (g + 1))
                if g >= 2:
                    act.wait_ge(S[f"ada_stored{g % 2}"], 64 * (g // 2))
                step(act.copy(modsb[:, g % 2, :, :].rearrange("p c n -> p (c n)"), banks[7][:, :]), "ada_copied")

            def root(ap, n, name):
                step(act.activation(ap, ap, ACT.Sqrt, scale=1.0 / n, bias=keep[:, KEEP["eps"]]), name)

            def squares(idx, ready):
                for t in range(NT):
                    ready(t)
                    step(act.activation(h[:, t, :], x[:, t, :], ACT.Square, accum_out=ss[:, t:t + 1]), "act_step",
                         hold=True)
                    root(ss[:, t:t + 1], D, "squares")

            def copy_transposed(idx):
                for t in range(NT):
                    for half in range(2):
                        n = 2 * (NT * idx + t) + half
                        act.wait_ge(S["trans_done"], n + 1)
                        step(act.copy(hT[:, 4 * half:4 * half + 4, t * P:t * P + P],
                                      banks[n % 2][:, :].rearrange("p (k n) -> p k n", k=4)), "trans_copied")

            def copy_projected(l):
                for g in range(PROJ0[l], PROJ0[l] + IN_CHUNKS[l] * NT):
                    if g % 2 == 0:
                        continue
                    c, t = divmod(g - PROJ0[l], NT)
                    w = min(512, IN_W[l] - 512 * c)
                    act.wait_ge(S["proj_done"], g + 1)
                    step(act.copy(qkv[l][:, t, 512 * c:512 * c + w], banks[2 + g % 4][:, 0:w]), "proj_copied_act")

            def mlstm():
                for t in range(NT):
                    act.wait_ge(S["bt_done"], 2 * t + 1)
                    step(act.copy(bqT[:, :, t * P:t * P + P], banks[3][:, :].rearrange("p (u s) -> p u s", u=4)),
                         "bt_copied_q")
                act.wait_ge(S["gates_in"], 1)
                step(act.activation(absf[:, :, :], absf[:, :, :], ACT.Exp, scale=-1.0), "gates_exp", hold=True)
                step(act.activation(absf[:, :, :], absf[:, :, :], ACT.Ln, bias=1.0), "gates_log")
                act.wait_ge(S["qk_squares"], 1)
                root(qss[:, :, :], HD, "qk_rooted")
                for s in range(3):
                    act.wait_ge(S["expo_ready"], s + 1)
                    step(act.activation(expo[:, :, :], expo[:, :, :], ACT.Exp), "expo_done")
                    act.wait_ge(S["wexp_ready"], s + 1)
                    step(act.activation(wexp[:, :, :], wexp[:, :, :], ACT.Exp), "wexp_done")
                    for d in range(2):
                        v = 2 * s + d
                        act.wait_ge(S["amatT_done"], v + 1)
                        if v:
                            act.wait_ge(S["bnum_done"], v)
                        step(act.copy(amatT[:, :, :].rearrange("p u s -> p (u s)"), banks[4][:, :]), "amatT_copied")
                act.wait_ge(S["hm_squares"], 1)
                root(hss[:, :, :], BD, "hm_rooted")
                for t in range(NT):
                    step(act.activation(qkv[0][:, t, BO:BO + 512], qkv[0][:, t, BO:BO + 512], ACT.Sigmoid),
                         "ogate_done")

            def attention(l):
                if l == 0:
                    act.wait_ge(S["state_stored"], 48)

                def copy_queries(j):
                    g = (0, NP[0])[l] + j
                    act.wait_ge(S["pair_done"], 2 * g + 1)
                    if j >= 2:
                        act.wait_ge(S["scores_done"], U0[l] + 6 * (j - 1))
                    step(act.mul(qT[:, g % 2, :], banks[5][:, 0:TOKENS], HD ** -0.5), "qT_copied")

                copy_queries(0)
                for i in range(NU[l] + 1):
                    if i % 6 == 3 and i // 6 + 1 < NP[l]:
                        copy_queries(i // 6 + 1)
                    if i < NU[l]:
                        j, t, hh = unit(l, i)
                        U = U0[l] + i
                        act.wait_ge(S["max_ready"], U + 1)
                        if U >= 2:
                            act.wait_ge(S["probT_done"], U - 1)
                        k0, k1 = keys_of(t)
                        step(act.activation(prob[:, U % 2, 0:k1 - k0], banks[U % 2][:, 0:k1 - k0], ACT.Exp,
                                            bias=negm[:, U % 4:U % 4 + 1], accum_out=lsum[:, U % 4:U % 4 + 1]),
                             "prob_ready")
                    if i >= 1:
                        U = U0[l] + i - 1
                        t = unit(l, i - 1)[1]
                        k0, k1 = keys_of(t)
                        act.wait_ge(S["probT_done"], U + 1)
                        if U >= 2:
                            act.wait_ge(S["pv_done"], U - 1)
                        step(act.copy(probT[:, U % 2, 0:k1 - k0], banks[2 + U % 2][:, 0:k1 - k0]), "probT_copied")
                    if l == 0 and i % 8 == 0 and i:
                        ada_copy(3 + i // 8 - 1)

            def copy_out_transposed(l):
                for t in range(NT):
                    for half in range(2):
                        n = 2 * (NT * l + t) + half
                        act.wait_ge(S["outT_done"], n + 1)
                        step(act.copy(hT[:, 4 * half:4 * half + 4, t * P:t * P + P],
                                      banks[n % 2][:, :].rearrange("p (k n) -> p k n", k=4)), "outT_copied")

            def route(l):
                act.wait_ge(S["route_exp"], 2 * l + 1)
                g4 = rt[:, 96:108]
                step(act.activation(g4, g4, ACT.Exp), "route_exped")
                act.wait_ge(S["route_exp"], 2 * l + 2)
                d3 = rt[:, 108:111]
                step(act.activation(d3, d3, ACT.Exp), "route_exped")

            def one(Q, e, u, base):
                def old(name):
                    if not (isinstance(e, int) and e + base < 2):
                        act.wait_ge(Q[name], e + (base - 1))

                act.wait_ge(Q["hid_done"], e + (base + 1))
                old("hidT_done")
                act.activation(hs[u][0:64, :], banks[2 + u][0:64, :], ACT.Silu).then_inc(Q["silu_done"], 1)
                act.wait_ge(Q["hidT_done"], e + (base + 1))
                old("hidT_ready")
                act.copy(upT[u][:, :, :], banks[4 + u][:, :].rearrange("p (k n) -> p k n", k=4)[:, :, 64:128])\
                    .then_inc(Q["upT_copied"], 1)
                act.wait_ge(Q["y_done"], e + (base + 1))
                if not (isinstance(e, int) and e + base < 2):
                    act.wait_ge(Q[f"scattered{u}"], gath(e, u, base) - 16)
                act.copy(ysb[u], banks[6 + u][:, :]).then_inc(Q["y_copied"], 1)

            def one_over(b, base):
                act.wait_ge(V["hid_done"], b + (base + 1))
                act.activation(hs[0][0:64, :], banks[2][0:64, :], ACT.Silu).then_inc(V["silu_done"], 1)
                act.wait_ge(V["hidT_done"], b + (base + 1))
                act.copy(upT[0][:, :, :], banks[4][:, :].rearrange("p (k n) -> p k n", k=4)[:, :, 64:128])\
                    .then_inc(V["upT_copied"], 1)
                act.wait_ge(V["y_done"], b + (base + 1))
                act.copy(ysb[0], banks[6][:, :]).then_inc(V["y_copied"], 1)

            def experts(l):
                base = l * EXPERTS
                one(M, 0, 0, base)
                one(M, 1, 1, base)
                with act.Fori(1, EXPERTS // 2) as i:
                    for u in range(2):
                        one(M, act.snap(i * 2 + u), u, base)
                act.wait_ge(S["over_ready"], l + 1)
                n_over = act.value_load(eid_i[0:1, OVER:OVER + 1], min_val=0, max_val=OVER)
                with act.If(n_over > 0):
                    act.wait_ge(M["scattered0"], 16 * (l + 1) * EXPERTS // 2)
                    with act.Fori(0, OVER) as b:
                        one_over(b, l * OVER)

            def scale_pairs(l):
                for t in range(NT):
                    act.wait_ge(S[f"pairs_loaded{t}"], 16 * (l + 1))
                    step(act.activation(pairs[:, t, 0, :], pairs[:, t, 0, :], ACT.Copy, scale=wtop[:, t, 0:1]),
                         "pair_scaled")

            for g in range(3):
                ada_copy(g)
            squares(0, lambda t: act.wait_ge(S["x_loaded" if t == 0 else "x_rest"], 16))
            for l in range(2):
                copy_transposed(2 * l)
                copy_projected(l)
                if l == 0:
                    mlstm()
                attention(l)
                copy_out_transposed(l)
                squares(2 * l + 1, lambda t: act.wait_ge(S["x_mixed"], 2 * (NT * l + t + 1)))
                copy_transposed(2 * l + 1)
                route(l)
                experts(l)
                scale_pairs(l)
                squares(2 * l + 2, lambda t: act.wait_ge(S["x_moe"], NT * l + t + 1))

        @block.vector
        def _(v):
            count = {}

            def do(ins, name="dve_step"):
                ins.then_inc(S[name], 1)
                count[name] = count.get(name, 0) + 1
                v.wait_ge(S[name], count[name])

            def tt(out, in0, in1, op, name="dve_step"):
                do(v.tensor_tensor(out, in0, in1, op), name)

            def ts(out, in0, s1, s2, op0, op1=None, name="dve_step"):
                do(v.tensor_scalar(out, in0, s1, s2, op0, op1) if op1 is not None else
                   v.tensor_scalar(out, in0, s1, s2, op0), name)

            def stt(out, in0, s, in1, op0, op1, name="dve_step"):
                do(v.scalar_tensor_tensor(out=out, in0=in0, scalar=s, in1=in1, op0=op0, op1=op1), name)

            def red(out, in_, op, name="dve_step"):
                do(v.tensor_reduce(out, in_, AX, op), name)

            def cp(out, in_, name="dve_step"):
                do(v.tensor_copy(out, in_), name)

            def last(ap, n):
                return ap.unsqueeze(len(ap.shape)).to_broadcast(list(ap.shape) + [n])

            def lead(ap, n):
                return ap.unsqueeze(1).to_broadcast([ap.shape[0], n] + list(ap.shape[1:]))

            v.wait_ge(S["cond_silu"], 1)
            for c in range(2):
                cp(cond32[:, :, 16 * c:16 * c + 16], last(condr[:, c, :], 16), "dve_step")
            do(v.memset(mstate[:, :], 0.0), "cond_rep")

            def modulation(l):
                v.wait_ge(S["cmod_loaded"], 80 * (l + 1))
                for c in range(2):
                    tt(cmod[:, c, :, :], cmod[:, c, :, :], cada[:, :, :], ALU.add)
                for c in range(2):
                    for k in range(2):
                        stt(cmod[:, c, 3 * k + 1, :], cmod[:, c, 3 * k + 1, :], 1.0, cgain[:, k, :], ALU.add, ALU.mult,
                            "cmod_ready")

            def normed(idx):
                for t in range(NT):
                    v.wait_ge(S["squares"], NT * idx + t + 1)
                    do(v.reciprocal(rstd[:, t:t + 1], ss[:, t:t + 1]))
                    if t == 0:
                        v.wait_ge(S["modAB_loaded"], 32 * (idx + 1))
                    c = 0 if t == 0 else 1
                    stt(h[:, t, :], x[:, t, :], rstd[:, t:t + 1], modA[:, c, :], ALU.mult, ALU.mult)
                    tt(h[:, t, :], h[:, t, :], modB[:, c, :], ALU.add, "h_ready")

            def copy_projected(l):
                for g in range(PROJ0[l], PROJ0[l] + IN_CHUNKS[l] * NT):
                    if g % 2:
                        continue
                    c, t = divmod(g - PROJ0[l], NT)
                    w = min(512, IN_W[l] - 512 * c)
                    v.wait_ge(S["proj_done"], g + 1)
                    cp(qkv[l][:, t, 512 * c:512 * c + w], banks[2 + g % 4][:, 0:w], "proj_copied_dve")

            def gate_logs():
                v.wait_ge(S["proj_copied_act"], AB_CHUNKS * NT // 2)
                v.wait_ge(S["small_loaded"], 16 * 6)
                tt(gates[:, :, :], qkv[0][:, :, BG:BG + 16], lead(gbias, NT), ALU.add)
                f = gates[:, :, :].rearrange("p t (d g h) -> p t d g h", d=2, g=2)
                ab = absf[:, :, :].rearrange("p t (d h) -> p t d h", d=2)
                for d in range(2):
                    stt(ab[:, :, d, :], f[:, :, d, 1, :], -1.0, f[:, :, d, 1, :], ALU.mult, ALU.max,
                        "dve_step" if d == 0 else "gates_in")
                v.wait_ge(S["gates_log"], 1)
                for s in range(3):
                    for d in range(2):
                        t = STAGES[s][d]
                        cols = slice(4 * d, 4 * d + 4)
                        cp(li[:, s, cols], f[:, t, d, 0, :])
                        stt(lf[:, s, cols], f[:, t, d, 1, :], 0.0, ab[:, t, d, :], ALU.min, ALU.subtract,
                            "dve_step" if 2 * s + d < 5 else "lf_ready")

            def head_norms():
                v.wait_ge(S["early_loaded"], 16)
                scratch = area_h[:, 0:640].rearrange("p (u s) -> p u s", u=QK_HEADS)
                for t in range(NT):
                    z = qkv[0][:, t, 0:AV].rearrange("p (u s) -> p u s", u=QK_HEADS)
                    tt(scratch, z, z, ALU.mult)
                    red(qss[:, t, :], scratch, ALU.add, "dve_step" if t < NT - 1 else "qk_squares")
                v.wait_ge(S["qk_rooted"], 1)
                do(v.reciprocal(qrs[:, :, :], qss[:, :, :]))
                for t in range(NT):
                    z = qkv[0][:, t, 0:AV].rearrange("p (u s) -> p u s", u=QK_HEADS)
                    tt(z, z, last(qrs[:, t, :], HD), ALU.mult)
                    tt(z, z, qkgain, ALU.mult, "qk_ready")
                    if t:
                        zz = z.rearrange("p u (b x c) -> p u b x c", b=2, x=2)
                        sc = scratch.rearrange("p u (b x c) -> p u b x c", b=2, x=2)
                        sn = early[:, EARLY["sin"]].rearrange("p (t b x c) -> p t b x c", t=2, b=2, x=2)
                        cs = early[:, EARLY["cos"]].rearrange("p (t c) -> p t c", t=2)
                        for b in range(2):
                            for y in range(2):
                                tt(sc[:, :, b, y, :], zz[:, :, b, 1 - y, :], lead(sn[:, t - 1, b, y, :], QK_HEADS),
                                   ALU.mult)
                        tt(z, z, lead(cs[:, t - 1, :], QK_HEADS), ALU.mult)
                        tt(z, z, scratch, ALU.add)

            def copy_b_keys():
                for t in range(NT):
                    v.wait_ge(S["bt_done"], 2 * t + 2)
                    cp(bkT[:, :, t * P:t * P + P], banks[4][:, :].rearrange("p (u s) -> p u s", u=4), "bt_copied_k")

            def mlstm():
                v.wait_ge(S["cum_done"], 1)
                sums = banks[0][:, 0:48].rearrange("p (s c) -> p s c", s=3)
                cp(bcum[:, :, :], sums[:, :, 0:8])
                cp(btot[:, :, :], sums[:, :, 8:16])
                tt(rrow[:, :, :], li[:, :, :], bcum[:, :, :], ALU.subtract)
                for s in range(3):
                    if s == 1:
                        v.wait_ge(S["state_loaded"], 48)
                    tt(diag[:, :, :], lead(ident, 8), last(rrow[:, s, :], P), ALU.mult, "diag_ready")
                    v.wait_ge(S["rows_done"], s + 1)
                    if s:
                        v.wait_ge(S["wexp_done"], s)
                    for d in range(2):
                        R = banks[1 + d][:, :].rearrange("p (u s) -> p u s", u=4)
                        red(gall[:, 4 * d:4 * d + 4], R, ALU.max)
                        tt(wexp[:, 4 * d:4 * d + 4, :], R, lead(early[:, EARLY["maskb" if d else "maskf"]], 4),
                           ALU.add)
                    red(gcol[:, :], wexp[:, :, :], ALU.max)
                    tt(gcol[:, :], gcol[:, :], mstate[:, :], ALU.max)
                    tt(gpick[:, :], gall[:, :], mstate[:, :], ALU.max)
                    tt(expo[:, 0, :], mstate[:, :], gcol[:, :], ALU.subtract)
                    tt(expo[:, 1, :], bcum[:, s, :], gcol[:, :], ALU.add)
                    ts(expo[:, 1, :], expo[:, 1, :], -1.0, None, ALU.mult)
                    tt(expo[:, 2, :], rrow[:, s, :], gpick[:, :], ALU.subtract)
                    tt(expo[:, 3, :], mstate[:, :], gpick[:, :], ALU.subtract, "expo_ready")
                    tt(wexp[:, :, :], wexp[:, :, :], last(gcol[:, :], P), ALU.subtract, "wexp_ready")
                    if s == 0:
                        tt(mout[:, :], btot[:, 0, :], gpick[:, :], ALU.add)
                        v.wait_ge(S["small_loaded"], 16 * 6)
                        cp(mstate[:, :], m0)
                    if s == 1:
                        tt(mstate[:, :], btot[:, 1, :], gpick[:, :], ALU.add)
                    v.wait_ge(S["wexp_done"], s + 1)
                    for d in range(2):
                        t = STAGES[s][d]
                        w = 2 * s + d
                        heads = slice(4 * d, 4 * d + 4)
                        v.wait_ge(S["bs_done"], w + 1)
                        if w:
                            v.wait_ge(S["amatT_done"], w)
                        stt(amat.rearrange("p u s -> p (u s)"), banks[3][:, :], BD ** -0.5,
                            wexp[:, heads, :].rearrange("p u s -> p (u s)"), ALU.mult, ALU.mult, "amat_ready")
                        red(dena[:, :], amat[:, :, :], ALU.add)
                        if s < 2:
                            if w:
                                v.wait_ge(S["bupd_done"], w)
                            kk = qkv[0][:, t, BK:BK + 512].rearrange("p (u s) -> p u s", u=4)
                            stt(kw, kk, BD ** -0.5, last(expo[:, 2, heads], P), ALU.mult, ALU.mult, "kw_ready")
                        v.wait_ge(S["bnum_done"], w + 1)
                        num = banks[5][:, :].rearrange("p (u s) -> p u s", u=4)
                        if s > 0:
                            qn = banks[1][:, 8 * d:8 * d + 4]
                            tt(den[:, :], qn, expo[:, 0, heads], ALU.mult)
                            tt(den[:, :], den[:, :], dena[:, :], ALU.add)
                            tt(tmp1, banks[6][:, :].rearrange("p (u s) -> p u s", u=4), last(expo[:, 0, heads], P),
                               ALU.mult)
                            tt(tmp1, tmp1, num, ALU.add)
                        else:
                            cp(den[:, :], dena[:, :])
                            cp(tmp1, num)
                        stt(den[:, :], den[:, :], -1.0, den[:, :], ALU.mult, ALU.max)
                        tt(den[:, :], den[:, :], expo[:, 1, heads], ALU.max)
                        do(v.reciprocal(den[:, :], den[:, :]))
                        out = hm[:, t, :].rearrange("p (u s) -> p u s", u=4)
                        first = (s == 0 and d == 0) or s == 1
                        if first:
                            tt(out, tmp1, last(den[:, :], BD), ALU.mult, "combined")
                        else:
                            tt(tmp1, tmp1, last(den[:, :], BD), ALU.mult)
                            tt(out, out, tmp1, ALU.add, "combined")
                        if s < 2:
                            v.wait_ge(S["bupd_done"], w + 1)
                            upd = banks[0][:, :].rearrange("p (u s) -> p u s", u=4)
                            nup = banks[2][:, 0:4]
                            if s == 0:
                                cp(nout[:, heads], nup)
                                cp(Cout[:, heads, :], upd, "cstate_ready")
                            else:
                                tt(Cst[:, heads, :], Cst[:, heads, :], last(expo[:, 3, heads], P), ALU.mult)
                                tt(nst[:, heads], nst[:, heads], expo[:, 3, heads], ALU.mult)
                                tt(nst[:, heads], nst[:, heads], nup, ALU.add)
                                tt(Cst[:, heads, :], Cst[:, heads, :], upd, ALU.add, "cstate_ready")
                for t in range(NT):
                    out = hm[:, t, :].rearrange("p (u s) -> p u s", u=4)
                    tt(tmp1, out, out, ALU.mult)
                    red(hss[:, t, :], tmp1, ALU.add, "dve_step" if t < NT - 1 else "hm_squares")
                v.wait_ge(S["hm_rooted"], 1)
                do(v.reciprocal(hss[:, :, :], hss[:, :, :]))
                for t in range(NT):
                    out = hm[:, t, :].rearrange("p (u s) -> p u s", u=4)
                    dst = qkv[0][:, t, BQ:BQ + 512].rearrange("p (u s) -> p u s", u=4)
                    tt(tmp1, out, last(hss[:, t, :], BD), ALU.mult)
                    tt(tmp1, tmp1, ogain, ALU.mult)
                    v.wait_ge(S["ogate_done"], t + 1)
                    tt(dst, tmp1, qkv[0][:, t, BO:BO + 512].rearrange("p (u s) -> p u s", u=4), ALU.mult,
                       "bout_ready")

            def duplicate_keys():
                for g in range(A_KV):
                    for s in range(4):
                        src = ctx_kv[:, 0, g * HD:g * HD + HD] if s == 1 else \
                            qkv[0][:, (0, None, 1, 2)[s], AK + g * HD:AK + g * HD + HD]
                        cp(kdup[:, g, s, :, :], lead(src, 2), "dve_step" if g * 4 + s < 7 else "kdup_ready")

            def window_bias():
                v.wait_ge(S["bias_loaded"], 16 * 2 * C_HEADS)
                for hh in range(C_HEADS):
                    tt(bias_na[:, hh, :, :], bias_na[:, hh, :, :], lead(keep[:, KEEP["window"]], 6), ALU.add,
                       "dve_step" if hh < C_HEADS - 1 else "bias_ready")

            def attention(l):
                def copy_keys(j):
                    g = (0, NP[0])[l] + j
                    v.wait_ge(S["pair_done"], 2 * g + 2)
                    if j >= 2:
                        v.wait_ge(S["scores_done"], U0[l] + 6 * (j - 1))
                    cp(kT[:, g % 2, :], banks[5][:, :], "kT_copied")

                copy_keys(0)
                for i in range(NU[l] + 3):
                    if i % 6 == 5 and i // 6 + 1 < NP[l]:
                        copy_keys(i // 6 + 1)
                    if i < NU[l]:
                        j, t, hh = unit(l, i)
                        U = U0[l] + i
                        k0, k1 = keys_of(t)
                        v.wait_ge(S["scores_done"], U + 1)
                        do(v.tensor_reduce(negm[:, U % 4:U % 4 + 1], banks[U % 2][:, 0:k1 - k0], AX, ALU.max,
                                           negate=True), "max_ready")
                    if i >= 3:
                        j, t, hh = unit(l, i - 3)
                        U = U0[l] + i - 3
                        v.wait_ge(S["pv_done"], U + 1)
                        col = U % 4
                        do(v.reciprocal(rlsum[:, col:col + 1], lsum[:, col:col + 1]))
                        c0 = (2 * j + hh) * HD
                        ts(qkv[l][:, t, c0:c0 + HD], banks[4 + 2 * (U % 2)][:, 0:HD],
                           rlsum[:, col:col + 1], None, ALU.mult, name="heads_out")

            def mix_in(l):
                v.wait_ge(S["modG_loaded"], 16 * (2 * l + 1))
                for t in range(NT):
                    for c in range(OUT_CHUNKS):
                        g = l * NT * OUT_CHUNKS + t * OUT_CHUNKS + c
                        cond = 0 if t == 0 else 1
                        v.wait_ge(S["out_done"], g + 1)
                        cols = slice(512 * c, 512 * c + 512)
                        tt(mixed[:, c, :], banks[2 + g % 2][:, :], modG[:, cond, cols], ALU.mult)
                        tt(x[:, t, cols], x[:, t, cols], mixed[:, c, :], ALU.add, "x_mixed")

            def route(l):
                r3 = lambda o, n: rt[:, o:o + 3 * n].rearrange("p (t n) -> p t n", t=NT)
                chosen, g4, d3 = r3(0, 32), r3(96, 4), rt[:, 108:111]
                lg, cg, og = r3(120, 36), r3(228, 4), r3(240, 4)
                gm, mn, gp = rt[:, 252:255], rt[:, 255:258], rt[:, 258:261]
                em, c32, o1, o2 = r3(264, 32), r3(360, 32), r3(456, 32), r3(552, 32)
                m1, m2, sl, fin = rt[:, 648:651], rt[:, 651:654], r3(656, 32), rt[:, 752:758]
                cnt, ex, ia, ib = rt[:, 760:792], rt[:, 792:824], rt[:, 824:856], rt[:, 856:888]
                iota = keep[:, KEEP["iota"]]

                def first_of(eq, width, onehot, top, logits):
                    tt(eq, logits, last(top, width), ALU.is_equal)
                    stt(eq, eq, -1000.0, lead(iota[:, 0:width], NT), ALU.mult, ALU.add)
                    red(mn, eq, ALU.min)
                    tt(onehot, eq, last(mn, width), ALU.is_equal)

                v.wait_ge(S["logits_done"], l + 1)
                v.wait_ge(S["kv_stored"], 32 * (l + 1))
                v.wait_ge(S["wge_loaded"], 32 * (l + 1))
                tt(lg, banks[6][:, 0:108].rearrange("p (t n) -> p t n", t=NT), lead(rbias, NT), ALU.add)
                red(gm, lg[:, :, 0:4], ALU.max)
                tt(g4, lg[:, :, 0:4], last(gm, 4), ALU.subtract, "route_exp")
                first_of(cg, 4, og, gm, lg[:, :, 0:4])
                ts(cg, og, FAR, -FAR, ALU.mult, ALU.add)
                for t in range(NT):
                    le = lg[:, t, 4:36].rearrange("p (g e) -> p g e", g=GROUPS)
                    emt = em[:, t, :].rearrange("p (g e) -> p g e", g=GROUPS)
                    tt(emt, le, last(og[:, t, :], PER_GROUP), ALU.mult)
                    tt(emt, emt, last(cg[:, t, :], PER_GROUP), ALU.add)
                red(m1, em, ALU.max)
                first_of(c32, 32, o1, m1, em)
                stt(em, o1, -3.0 * FAR, em, ALU.mult, ALU.add)
                red(m2, em, ALU.max)
                first_of(c32, 32, o2, m2, em)
                tt(d3, m2, m1, ALU.subtract, "route_exp")
                tt(chosen, o1, o2, ALU.add, "chosen")
                v.wait_ge(S["route_exped"], 2 * l + 2)
                red(gp, g4, ALU.add)
                stt(gm, d3, 1.0, gp, ALU.add, ALU.mult)
                do(v.reciprocal(wtop[:, :, 0], gm))
                tt(wtop[:, :, 1], wtop[:, :, 0], d3, ALU.mult)
                v.wait_ge(S["ranks_done"], l + 1)
                tt(sl, banks[0][:, 0:96].rearrange("p (t n) -> p t n", t=NT), chosen, ALU.subtract)
                cp(cnt, banks[0][:, 96:128])
                ts(ex, cnt, float(BLOCK), None, ALU.is_gt)
                for m in range(2, TOKENS // BLOCK):
                    stt(ex, cnt, float(BLOCK * m), ex, ALU.is_gt, ALU.add)
                cp(ia, ex)
                src, dst = ia, ib
                for sh in (1, 2, 4, 8, 16):
                    cp(dst[:, 0:sh], src[:, 0:sh])
                    tt(dst[:, sh:32], src[:, sh:32], src[:, 0:32 - sh], ALU.add)
                    src, dst = dst, src
                nb = OVER
                grid = rt[:, 264:264 + nb * 32].rearrange("p (b e) -> p b e", b=nb)
                cp(o1_keep, o1)
                cp(o2_keep, o2)
                tt(grid, lead(src, nb), last(iota[:, 0:nb], 32), ALU.is_le)
                red(fin2, grid, ALU.add)
                ts(eid_i[:, 0:nb], fin2, float(EXPERTS - 1), None, ALU.min)
                cp(eid_i[:, nb:nb + 1], src[:, 31:32], "over_ready")
                tt(dst, src, ex, ALU.subtract)
                ts(dst, dst, float(BLOCK), float(BLOCK * (EXPERTS - 1)), ALU.mult, ALU.add)
                tt(dst, dst, keep[:, KEEP["first"]], ALU.subtract)
                ge = r3(264, 32)
                ts(ge, sl2, float(BLOCK), None, ALU.is_ge)
                tt(ge, ge, lead(dst, NT), ALU.mult)
                tt(sl2, sl2, ge, ALU.add)
                tt(sl2, sl2, lead(keep[:, KEEP["first"]], NT), ALU.add)
                for k, oh in enumerate((o1_keep, o2_keep)):
                    tt(oh, oh, sl2, ALU.mult)
                    red(fin2[:, 0:3], oh, ALU.add)
                    cp(slot_u[:, k, :], fin2[:, 0:3], "slots_ready")
                v.wait_ge(S["slots_loaded"], 32 * (l + 1))
                ts(slots_i, slots_f, keep[:, KEEP["half"]], None, ALU.add, name="index_ready")

            rbias = rbias_sb[:, :]
            m0 = m0_sb[:, :]
            fin2 = area_q[:, 3300:3300 + OVER]
            o1_keep = area_q[:, 3328:3424].rearrange("p (t n) -> p t n", t=NT)
            o2_keep = area_q[:, 3424:3520].rearrange("p (t n) -> p t n", t=NT)
            sl2 = rt[:, 656:752].rearrange("p (t n) -> p t n", t=NT)

            def one(Q, e, u, base):
                def old(name):
                    if not (isinstance(e, int) and e + base < 2):
                        v.wait_ge(Q[name], e + (base - 1))

                v.wait_ge(Q["hid_done"], e + (base + 1))
                old("hidT_done")
                v.tensor_copy(hs[u][64:128, :], banks[2 + u][64:128, :]).then_inc(Q["up_copied"], 1)

            def tokens(Q, e, u, base):
                v.wait_ge(Q["xT_done"], e + (base + 1))
                if not (isinstance(e, int) and e + base < 2):
                    v.wait_ge(Q["hid_done"], e + (base - 1))
                v.tensor_copy(xT[u][:, :, :].rearrange("p k s -> p (k s)"), banks[u][:, :]).then_inc(Q["xT_copied"], 1)

            def product(Q, e, u, base):
                v.wait_ge(Q["upT_copied"], e + (base + 1))
                if not (isinstance(e, int) and e + base < 2):
                    v.wait_ge(Q["y_done"], e + (base - 1))
                v.tensor_tensor(hidT[u][:, :, :], banks[4 + u][:, :].rearrange("p (k n) -> p k n", k=4)[:, :, 0:64],
                                upT[u][:, :, :], ALU.mult).then_inc(Q["hidT_ready"], 1)

            def experts(l):
                base = l * EXPERTS

                def whole(e, u, lastone):
                    one(M, e, u, base)
                    if not lastone:
                        tokens(M, e + 1, 1 - u, base)
                    product(M, e, u, base)

                tokens(M, 0, 0, base)
                whole(0, 0, False)
                whole(1, 1, False)
                with v.Fori(1, EXPERTS // 2 - 1) as i:
                    for u in range(2):
                        whole(v.snap(i * 2 + u), u, False)
                whole(EXPERTS - 2, 0, False)
                whole(EXPERTS - 1, 1, True)
                v.wait_ge(S["over_ready"], l + 1)
                n_over = v.value_load(eid_i[0:1, OVER:OVER + 1], min_val=0, max_val=OVER)
                with v.If(n_over > 0):
                    with v.Fori(0, OVER) as b:
                        bb = l * OVER
                        v.wait_ge(V["xT_done"], b + (bb + 1))
                        v.tensor_copy(xT[0][:, :, :].rearrange("p k s -> p (k s)"), banks[0][:, :])\
                            .then_inc(V["xT_copied"], 1)
                        v.wait_ge(V["hid_done"], b + (bb + 1))
                        v.tensor_copy(hs[0][64:128, :], banks[2][64:128, :]).then_inc(V["up_copied"], 1)
                        v.wait_ge(V["upT_copied"], b + (bb + 1))
                        v.tensor_tensor(hidT[0][:, :, :],
                                        banks[4][:, :].rearrange("p (k n) -> p k n", k=4)[:, :, 0:64],
                                        upT[0][:, :, :], ALU.mult).then_inc(V["hidT_ready"], 1)

            def combine(l):
                v.wait_ge(S["modG_loaded"], 16 * (2 * l + 2))
                for t in range(NT):
                    c = 0 if t == 0 else 1
                    v.wait_ge(S["pair_scaled"], NT * l + t + 1)
                    y = pairs[:, t, 0, :]
                    stt(y, pairs[:, t, 1, :], wtop[:, t, 1:2], y, ALU.mult, ALU.add)
                    tt(y, y, modG[:, c, :], ALU.mult)
                    tt(x[:, t, :], x[:, t, :], y, ALU.add, "x_moe")

            modulation(0)
            for l in range(2):
                normed(2 * l)
                copy_projected(l)
                if l == 0:
                    copy_b_keys()
                    gate_logs()
                    head_norms()
                    mlstm()
                    v.wait_ge(S["small_loaded"], 16 * 6)
                    duplicate_keys()
                else:
                    window_bias()
                attention(l)
                if l == 0:
                    modulation(1)
                mix_in(l)
                normed(2 * l + 1)
                route(l)
                experts(l)
                combine(l)
            v.wait_ge(S["gfin_loaded"], 16)
            for t in range(NT):
                v.wait_ge(S["squares"], NT * 4 + t + 1)
                do(v.reciprocal(rstd[:, t:t + 1], ss[:, t:t + 1]))
                stt(h[:, t, :], x[:, t, :], rstd[:, t:t + 1], modA[:, 0, :], ALU.mult, ALU.mult, "y_ready")

        @block.gpsimd
        def _(pool):
            def get(dst, src, name, tiny=False):
                pool.dma_start(dst, src, allow_slow_non_contiguous=tiny).then_inc(S[name], 16)

            def spread(ap, n=P):
                return ap.unsqueeze(0).to_broadcast([n] + list(ap.shape))

            def store_ada(l, g):
                G = 3 * l + g
                pool.wait_ge(S["ada_copied"], G + 1)
                dst = mod_dram[l].rearrange("c (v j n) -> c v j n", v=ADA_CHUNKS, j=4)
                for j in range(4):
                    pool.dma_start(dst[:, 4 * g:4 * g + 4, j, :], modsb[32 * j:32 * j + 32:16, G % 2, :, :])\
                        .then_inc(S[f"ada_stored{G % 2}"], 16)

            def finish_mod(l):
                pool.wait_ge(S["ada_stored0"], 64 * (2, 3)[l])
                pool.wait_ge(S["ada_stored1"], 64 * (1, 3)[l])
                for c in range(2):
                    get(cmod[:, c, :, :], mod_dram[l, c].rearrange("(v p i) -> p v i", v=6, p=P), "cmod_loaded")
                get(cada[:, :, :], a["ada_b"][l].rearrange("(v p i) -> p v i", v=6, p=P), "cmod_loaded")
                get(cgain[:, 0, :], a["norm_mix"][l].rearrange("(p i) -> p i", p=P), "cmod_loaded")
                get(cgain[:, 1, :], a["norm_ffn"][l].rearrange("(p i) -> p i", p=P), "cmod_loaded")
                pool.wait_ge(S["cmod_ready"], 4 * (l + 1))
                for c in range(2):
                    get(modf_dram[l, :, c, :].rearrange("v (p i) -> p v i", p=P), cmod[:, c, :, :], "cmod_stored")

            def load_AB(l, which):
                get(modA[:, :, :], spread(modf_dram[l, 3 * which + 1]), "modAB_loaded")
                get(modB[:, :, :], spread(modf_dram[l, 3 * which]), "modAB_loaded")

            def load_G(l, which):
                get(modG[:, :, :], spread(modf_dram[l, 3 * which + 2]), "modG_loaded")

            get(keep[:, :], a["keep"], "keep_loaded")
            get(condr[:, 0, :], a["c_ctx"].rearrange("(p k) -> p k", p=P), "cond_loaded")
            get(condr[:, 1, :], a["c"][0].rearrange("(p k) -> p k", p=P), "cond_loaded")
            get(x[:, 1:NT, :], a["x_sample"][0].rearrange("(t p) d -> p t d", p=P), "x_rest")
            get(x[:, 0, :], a["x_prompt"][0], "x_loaded")
            get(early, a["early"], "early_loaded")
            clear = area_t[:, 0:2 * SLOTS // P]
            pool.memset(clear, SKIP).then_inc(S["table_filled"], 1)
            pool.wait_ge(S["table_filled"], 1)
            for l in range(2):
                get(slot_dram[l].rearrange("s v -> (s v)").rearrange("(p n) -> p n", p=P), clear, "table_cleared")
            pool.wait_ge(S["table_cleared"], 32)
            for g in range(3):
                store_ada(0, g)
            finish_mod(0)
            pool.wait_ge(S["cmod_stored"], 32)
            load_AB(0, 0)
            pool.wait_ge(S["h_ready"], NT)
            gv = a["ab_q_norm"][0]
            get(qkgain[:, 0:A_HEADS, :], gv.unsqueeze(0).unsqueeze(0).to_broadcast([P, A_HEADS, HD]), "small_loaded")
            get(qkgain[:, A_HEADS:QK_HEADS, :],
                a["ab_k_norm"][0].unsqueeze(0).unsqueeze(0).to_broadcast([P, A_KV, HD]), "small_loaded")
            get(gbias, spread(a["ab_gate_bias"][0].rearrange("g h -> (g h)")), "small_loaded")
            get(ogain, spread(a["ab_out_norm"][0]), "small_loaded")
            get(m0_sb[:, :], spread(a["state_mlstm_m"][0, 0].rearrange("d h -> (d h)")), "small_loaded")
            for v2, src in enumerate((a["cache_attn_k"], a["cache_attn_v"])):
                get(ctx_kv[:, v2, :], src[0, 0].rearrange("t g d -> t (g d)"), "small_loaded" if v2 == 0 else "ctx_v")
            get(Cst[:, 0:4, :], a["state_mlstm_C"][0, 0, 0].rearrange("h d e -> d h e"), "state_loaded")
            get(Cst[:, 4:8, :], a["state_mlstm_C"][0, 0, 1].rearrange("h d e -> d h e"), "state_loaded")
            get(nst[:, :], a["state_mlstm_n"][0, 0].rearrange("d h e -> e (d h)"), "state_loaded", True)
            pool.wait_ge(S["qk_ready"], 1)
            for dst, c0 in ((o["new_attn_k"], AK), (o["new_attn_v"], AV)):
                get(dst[0, 0].rearrange("t g d -> t (g d)"), qkv[0][:, 0, c0:c0 + A_KV * HD], "kv_stored")
            pool.wait_ge(S["cstate_ready"], 2)
            get(o["new_mlstm_C"][0, 0].rearrange("d h e f -> e (d h) f"), Cout[:, :, :], "state_stored")
            get(o["new_mlstm_n"][0, 0].rearrange("d h e -> e (d h)"), nout[:, :], "state_stored", True)
            get(o["new_mlstm_m"][0, 0].rearrange("d h -> (d h)").unsqueeze(0), mout[0:1, :], "state_stored")
            pool.wait_ge(S["state_stored"], 48)

            def gather(Q, e, u, base, l):
                if not (isinstance(e, int) and e + base < 2):
                    pool.wait_ge(Q["xT_done"], e + (base - 1))
                pool.indirect_dma_start(out=xg[u], out_offset=None, in_=h2_dram[l],
                                        in_offset=bass.IndirectOffsetOnAxis(ap=slot_col(e, 0), axis=0),
                                        bounds_check=2 * TOKENS - 1, oob_is_err=False)\
                    .then_inc(Q[f"gathered{u}"], 16)

            def scatter(Q, e, u, base, l):
                pool.wait_ge(Q["y_copied"], e + (base + 1))
                pool.indirect_dma_start(out=pair_dram[l], in_=ysb[u], in_offset=None,
                                        out_offset=bass.IndirectOffsetOnAxis(ap=slot_col(e, 1), axis=0),
                                        bounds_check=2 * PAIRS - 1, oob_is_err=False)\
                    .then_inc(Q[f"scattered{u}"], 16)

            def slot_col(e, k):
                return slots_i[:, e, k:k + 1] if isinstance(e, int) else \
                    slots_i[:, bass.ds(e, 1), k:k + 1].rearrange("p a b -> p (a b)")

            for l in range(2):
                if l == 1:
                    pool.wait_ge(S["h_ready"], NT * 3)
                    for hh in range(C_HEADS):
                        for rr in range(2):
                            src = bass.AP(a["rpb"].tensor, (hh * 7 + 1 - rr) * 127, [[1, GRID_W], [127, 6], [1, GRID_W]])
                            get(bias_na[64 * rr:64 * rr + 64, hh, :, :], src, "bias_loaded")
                    pool.wait_ge(S["proj_done"], PROJ0[1] + NA_CHUNKS * NT)
                    for v2, src in enumerate((a["cache_na_k"], a["cache_na_v"])):
                        get(na_ctx[:, v2, :], src[0, 0].rearrange("t h d -> t (h d)"), "na_ctx_loaded")
                    for name in ("proj_copied_dve", "proj_copied_act"):
                        pool.wait_ge(S[name], (PROJ0[1] + NA_CHUNKS * NT) // 2)
                    for dst, c0 in ((o["new_na_k"], D), (o["new_na_v"], 2 * D)):
                        get(dst[0, 0].rearrange("t h d -> t (h d)"), qkv[1][:, 0, c0:c0 + D], "kv_stored")
                if l == 0:
                    for g in range(3):
                        store_ada(1, g)
                pool.wait_ge(S["heads_out"], U0[l] + NU[l])
                load_G(l, 0)
                load_AB(l, 1)
                wv = a["moe_wg"][l].rearrange("(k p) n -> p k n", p=P)
                get(wge[:, :, 0:GROUPS], wv, "wge_w")
                get(wge[:, :, GROUPS:], a["moe_we"][l].rearrange("(k p) n -> p k n", p=P), "wge_w")
                get(rbias_sb[:, 0:GROUPS], spread(a["moe_bg"][l]), "wge_loaded")
                get(rbias_sb[:, GROUPS:], spread(a["moe_be"][l]), "wge_loaded")
                if l == 0:
                    finish_mod(1)
                pool.wait_ge(S["h_ready"], NT * (2 * l + 2))
                get(h2_dram[l].rearrange("(t p c) d -> p t (c d)", p=P, c=2), h[:, :, :], "h2_stored")
                pool.wait_ge(S["x_mixed"], NT * OUT_CHUNKS * (l + 1))
                load_G(l, 1)
                pool.wait_ge(S["slots_ready"], 2 * (l + 1))
                for t in range(NT):
                    for k in range(2):
                        val = keep[:, KEEP["tok"].start + 4 * t + 2 * k:KEEP["tok"].start + 4 * t + 2 * k + 2]
                        pool.indirect_dma_start(out=slot_dram[l], in_=val, in_offset=None,
                                                out_offset=bass.IndirectOffsetOnAxis(ap=slot_u[:, k, t:t + 1], axis=0))\
                            .then_inc(S["slots_scattered"], 16)
                pool.memset(area_t[:, 0:1024], 0.0).then_inc(S["xg_cleared"], 1)
                pool.wait_ge(S["slots_scattered"], 96 * (l + 1))
                for half in range(2):
                    get(slots_f[64 * half:64 * half + 64, :, :],
                        slot_dram[l].rearrange("(e s) v -> s e v", s=BLOCK), "slots_loaded")
                pool.wait_ge(S["index_ready"], l + 1)
                pool.wait_ge(S["h2_stored"], 16 * (l + 1))
                pool.wait_ge(S["xg_cleared"], l + 1)
                base = l * EXPERTS
                gather(M, 0, 0, base, l)
                gather(M, 1, 1, base, l)
                for e in range(EXPERTS):
                    if e + 2 < EXPERTS:
                        gather(M, e + 2, e % 2, base, l)
                    scatter(M, e, e % 2, base, l)
                n_over = pool.value_load(eid_i[0:1, OVER:OVER + 1], min_val=0, max_val=OVER)
                with pool.If(n_over > 0):
                    for b in range(OVER):
                        B = b + l * OVER
                        if b:
                            pool.wait_ge(V["xT_done"], B)
                        pool.indirect_dma_start(out=xg[0], out_offset=None, in_=h2_dram[l],
                                                in_offset=bass.IndirectOffsetOnAxis(ap=slot_col(EXPERTS + b, 0), axis=0),
                                                bounds_check=2 * TOKENS - 1, oob_is_err=False)\
                            .then_inc(V["gathered0"], 16)
                        pool.wait_ge(V["y_copied"], B + 1)
                        pool.indirect_dma_start(out=pair_dram[l], in_=ysb[0], in_offset=None,
                                                out_offset=bass.IndirectOffsetOnAxis(ap=slot_col(EXPERTS + b, 1), axis=0),
                                                bounds_check=2 * PAIRS - 1, oob_is_err=False)\
                            .then_inc(V["scattered0"], 16)
                        pool.wait_ge(V["scattered0"], 16 * (B + 1))
                for u in range(2):
                    pool.wait_ge(M[f"scattered{u}"], 16 * (l + 1) * EXPERTS // 2)
                for t in range(NT):
                    get(pairs[:, t, :, :].rearrange("p k d -> p (k d)"),
                        pair_dram[l].rearrange("(t p c) d -> t p (c d)", t=NT, p=P)[t], f"pairs_loaded{t}")
                if l == 0:
                    pool.wait_ge(S["cmod_stored"], 64)
                    load_AB(1, 0)
                else:
                    get(modA[:, 0, :], spread(a["norm_final"]), "gfin_loaded")
            for t in range(NT):
                pool.wait_ge(S["y_ready"], t + 1)
                dst = o["y_prompt"][0] if t == 0 else o["y_sample"][0, (t - 1) * P:t * P, :]
                get(dst, h[:, t, :], "y_stored")
            pool.wait_ge(S["y_stored"], 16 * NT)
            pool.wait_ge(S["kv_stored"], 64)
            pool.wait_ge(S["state_stored"], 48)


_OUTS = [("y_prompt", (1, SEQ, D)), ("y_sample", (1, DEC_SEQ, D)), ("new_attn_k", (1, 1, SEQ, A_KV, HD)),
         ("new_attn_v", (1, 1, SEQ, A_KV, HD)), ("new_mlstm_C", (1, 1, 2, B_HEADS, BD, BD)),
         ("new_mlstm_n", (1, 1, 2, B_HEADS, BD)), ("new_mlstm_m", (1, 1, 2, B_HEADS)),
         ("new_na_k", (1, 1, SEQ, C_HEADS, HD)), ("new_na_v", (1, 1, SEQ, C_HEADS, HD))]


def kernel(**inputs):
    import concourse.bacc as _bacc
    from concourse.bass_utils import run_bass_kernel_spmd as _run

    nc = _bacc.Bacc("TRN2", target_bir_lowering=False, num_devices=1)
    arrays, aps = {}, {}
    inputs = {k: np.asarray(v) for k, v in inputs.items()}
    rpb = inputs.pop("na_rpb")[0]
    reach = ROWS - 1
    padded = np.zeros((C_HEADS, 2 * ROWS - 1, 2 * GRID_W - 1), rpb.dtype)
    mid = GRID_W - NA_COLS
    padded[:, :, mid:mid + 2 * NA_COLS - 1] = rpb[:, NA_ROWS_MAX - 1 - reach:NA_ROWS_MAX + reach]
    inputs["rpb"] = padded
    inputs["keep"], inputs["early"] = tables()
    for name, value in inputs.items():
        value = np.ascontiguousarray(value)
        arrays[f"in_{name}"] = value
        aps[name] = nc.dram_tensor(f"in_{name}", value.shape, mybir.dt.from_np(value.dtype), kind="ExternalInput").ap()
    outs = {n: nc.dram_tensor(f"out_{n}", s, F32, kind="ExternalOutput").ap() for n, s in _OUTS}
    build(nc, aps, outs)
    r = _run(nc, [arrays], core_ids=[0])
    return tuple(r.results[0][f"out_{n}"] for n, _ in _OUTS)
```

```python
from contextlib import ExitStack

import numpy as np

import concourse.bass as bass
from concourse import mybir

P = 128
D = 1024
KT = D // P
SEQ, DEC_SEQ, PAST = 128, 256, 128
NT = (SEQ + DEC_SEQ) // P
TOKENS = NT * P
GRID_W = 64
ROWS = DEC_SEQ // GRID_W
A_HEADS, A_KV, HD = 8, 2, 64
B_HEADS, BD = 4, 128
C_HEADS = 16
NA_ROWS_MAX, NA_COLS = 8, 16
AB_W = A_HEADS * HD + 2 * A_KV * HD + 4 * B_HEADS * BD + 4 * B_HEADS
NA_W = 3 * C_HEADS * HD
AQ, AK, AV = 0, A_HEADS * HD, A_HEADS * HD + A_KV * HD
BQ = AV + A_KV * HD
BK, BV, BO = BQ + B_HEADS * BD, BQ + 2 * B_HEADS * BD, BQ + 3 * B_HEADS * BD
BG = BO + B_HEADS * BD
QK_HEADS = A_HEADS + A_KV
GROUPS, PER_GROUP = 4, 8
EXPERTS = GROUPS * PER_GROUP
FF = 512
BLOCK = 64
OVER = (2 * TOKENS - 1) // BLOCK
PAIRS = 2 * TOKENS
EPS = 1e-6
FAR = 1.0e30
SKIP = 1.0e5

RING = 6
CHUNK = 4096
ADA_CHUNKS = 6 * D // 512
AB_CHUNKS = (AB_W + 511) // 512
NA_CHUNKS = NA_W // 512
OUT_CHUNKS = D // 512

F32 = mybir.dt.float32
I32 = mybir.dt.int32
U32 = mybir.dt.uint32
ALU = mybir.AluOpType
ACT = mybir.ActivationFunctionType
AX = mybir.AxisListType.X

KEEP = {}
_at = 0
for _name, _n in (("ident", 128), ("trif", 128), ("ones", 128), ("flip", 128), ("window", 64),
                  ("slot", 128), ("skip", 1), ("eps", 1), ("pair", 3)):
    KEEP[_name] = slice(_at, _at + _n)
    _at += _n
NKEEP = _at
EARLY = {}
_at = 0
for _name, _n in (("trib", 128), ("maskf", 128), ("maskb", 128), ("cos", 128), ("sin", 128)):
    EARLY[_name] = slice(_at, _at + _n)
    _at += _n
NEARLY = _at


def tables():
    keep = np.zeros((P, NKEEP), np.float32)
    early = np.zeros((P, NEARLY), np.float32)
    p = np.arange(P)
    keep[:, KEEP["ident"]] = np.eye(P)
    keep[:, KEEP["trif"]] = p[:, None] <= p[None, :]
    keep[:, KEEP["ones"]] = 1.0
    col = p % GRID_W
    mirror = p - col + GRID_W - 1 - col
    keep[p, KEEP["flip"].start + mirror] = 1.0
    c = GRID_W - 1 - col
    start = np.clip(c - NA_COLS // 2, 0, GRID_W - NA_COLS)
    k = np.arange(GRID_W)
    inside = (k[None, :] >= start[:, None]) & (k[None, :] < start[:, None] + NA_COLS)
    keep[:, KEEP["window"]] = np.where(inside, 0.0, -FAR)
    keep[:, KEEP["slot"]] = np.arange(P) % BLOCK
    keep[:, KEEP["skip"]] = SKIP + (p >= BLOCK)[:, None]
    keep[:, KEEP["eps"]] = EPS
    keep[:, KEEP["pair"]] = 4 * (np.arange(NT)[None] * P + p[:, None]) - SKIP
    early[:, EARLY["trib"]] = p[:, None] >= p[None, :]
    early[:, EARLY["maskf"]] = np.where(p[:, None] >= p[None, :], 0.0, -FAR)
    early[:, EARLY["maskb"]] = np.where(p[:, None] <= p[None, :], 0.0, -FAR)
    half = HD // 2
    freqs = 1.0 / (10000.0 ** (np.arange(0, half, 2, dtype=np.float32) / half))
    tok = np.arange(DEC_SEQ)
    rot = []
    for pos in (tok // GRID_W, tok % GRID_W):
        rot.append(pos[:, None].astype(np.float32) * freqs[None, :])
    cos = np.concatenate([np.cos(rot[0]), np.cos(rot[0]), np.cos(rot[1]), np.cos(rot[1])], -1)
    sin = np.concatenate([-np.sin(rot[0]), np.sin(rot[0]), -np.sin(rot[1]), np.sin(rot[1])], -1)
    early[:, EARLY["cos"]] = cos.reshape(2, P, HD).transpose(1, 0, 2).reshape(P, 2 * HD)
    early[:, EARLY["sin"]] = sin.reshape(2, P, HD).transpose(1, 0, 2).reshape(P, 2 * HD)
    return keep, early


def build(nc, a, o):
    ctx = ExitStack()
    with ctx:
        def sb(name, shape, dt=F32):
            return ctx.enter_context(nc.sbuf_tensor(name, shape, dt))

        def sem(name):
            return ctx.enter_context(nc.semaphore(name))

        ring = sb("ring", [P, RING, CHUNK])
        x = sb("x", [P, NT, D])
        area_h = sb("area_h", [P, 3 * D])
        area_t = sb("area_t", [P, 3 * D])
        area_q = sb("area_q", [P, NT * NA_W])
        area_m = sb("area_m", [P, 6144])
        area_g = sb("area_g", [P, 2 * D])
        keep = sb("keep", [P, NKEEP])
        wge = sb("wge", [P, KT, GROUPS + EXPERTS])
        ctx_kv = sb("ctx_kv", [P, 2, A_KV * HD])
        condr = sb("condr", [P, 2, KT])
        cond32 = sb("cond32", [P, KT, 32])
        small = sb("small", [P, 444])
        used = [0]

        def small_cut(*shape):
            n = int(np.prod(shape))
            v = small[:, used[0]:used[0] + n]
            used[0] += n
            if len(shape) == 2:
                v = v.rearrange("p (a b) -> p a b", a=shape[0])
            if len(shape) == 3:
                v = v.rearrange("p (a b c) -> p a b c", a=shape[0], b=shape[1])
            return v

        psum = ctx.enter_context(nc.psum_tensor("psum", [P, 8, 512], F32))
        banks = [psum[:, i, :] for i in range(8)]
        mod_dram = nc.dram_tensor("mod_raw", [2, 2, 6 * D], F32).ap()
        modf_dram = nc.dram_tensor("mod_ready", [2, 6, 2, D], F32).ap()
        pair_dram = [nc.dram_tensor(f"pair_rows{l}", [2 * PAIRS, D // 2], F32).ap() for l in range(2)]

        ident, trif, ones, flip = (keep[:, KEEP[n]] for n in ("ident", "trif", "ones", "flip"))
        h = area_h[:, :].rearrange("p (t d) -> p t d", t=NT)
        hT = area_t[:, :].rearrange("p (k n) -> p k n", k=KT)
        qkv = [area_q[:, 0:NT * AB_W].rearrange("p (t n) -> p t n", t=NT),
               area_q[:, :].rearrange("p (t n) -> p t n", t=NT)]
        early = area_q[:, NT * AB_W:NT * AB_W + NEARLY]
        modA = area_m[:, 0:2 * D].rearrange("p (c d) -> p c d", c=2)
        modB = area_m[:, 2 * D:4 * D].rearrange("p (c d) -> p c d", c=2)
        modG = area_g[:, :].rearrange("p (c d) -> p c d", c=2)
        bias_row = area_q[0:1, 0:2 * D]
        first_gain = area_g[:, 0:D]
        modsb = area_m[:, 5120:6144].rearrange("p (b c n) -> p b c n", b=2, c=4)
        cada = area_m[:, 4752:4848].rearrange("p (l v i) -> p l v i", l=2, v=6)
        cgain = area_m[:, 4848:4880].rearrange("p (l v i) -> p l v i", l=2, v=2)
        cmod = area_m[:, 4880:4944].rearrange("p (b c v i) -> p b c v i", b=2, c=2, v=2)
        hm = area_h[:, 0:NT * 512].rearrange("p (t n) -> p t n", t=NT)
        wexp = [v.rearrange("p (u s) -> p u s", u=8) for v in (area_h[:, 1536:2560], area_m[:, 0:1024])]
        amat = [v.rearrange("p (u s) -> p u s", u=4) for v in (area_h[:, 2560:3072], area_g[:, 1024:1536])]
        bqT = area_t[:, 0:1536].rearrange("p (h n) -> p h n", h=4)
        bkT = area_t[:, 1536:3072].rearrange("p (h n) -> p h n", h=4)
        amatT = area_m[:, 1024:1536].rearrange("p (u s) -> p u s", u=4)
        tmp1 = area_m[:, 1536:2048].rearrange("p (u s) -> p u s", u=4)
        kw = [v.rearrange("p (u s) -> p u s", u=4) for v in (area_m[:, 2048:2560], area_g[:, 1536:2048])]
        Cst = area_m[:, 2560:3584].rearrange("p (u s) -> p u s", u=8)
        qkgain = area_m[:, 3584:4224].rearrange("p (u s) -> p u s", u=QK_HEADS)
        ogain = area_m[:, 4224:4736].rearrange("p (u s) -> p u s", u=4)
        gbias = area_m[:, 4736:4752]
        m0_sb = area_m[:, 4944:4952]
        Cout = area_g[:, 0:1024].rearrange("p (u s) -> p u s", u=8)
        kdup = area_m[:, 0:1024].rearrange("p (v s x c) -> p v s x c", v=A_KV, s=4, x=2)
        prob = area_g[:, 0:1536].rearrange("p (b h n) -> p b h n", b=2, h=2)
        probT = [area_t[:, o:o + 768].rearrange("p (h n) -> p h n", h=2) for o in (2048, 1024)]
        qT = [v.rearrange("p (b n) -> p b n", b=2) for v in (area_h[:, 1536:2304], area_h[:, 0:768])]
        kT = [v.rearrange("p (b n) -> p b n", b=2) for v in (area_t[:, 0:1024], area_h[:, 768:1792])]
        na_k = area_h[:, 1792:2816]
        na_v = area_t[:, 0:D]
        bias_na = area_m[:, :].rearrange("p (h r c) -> p h r c", h=C_HEADS, r=6)
        mixed = area_m[:, 4608:5632].rearrange("p (b n) -> p b n", b=2)
        sel = [area_t[:, 384 * i:384 * i + 384].rearrange("p (t s) -> p t s", t=NT) for i in range(2)]
        xT = [area_t[:, 1024 + 512 * i:1536 + 512 * i].rearrange("p (k s) -> p k s", k=4) for i in range(2)]
        hidT = [area_t[:, 2048 + 256 * i:2304 + 256 * i].rearrange("p (k s) -> p k s", k=4) for i in range(2)]
        upT = [area_t[:, 2560 + 256 * i:2816 + 256 * i].rearrange("p (k s) -> p k s", k=4) for i in range(2)]
        tok = area_q[:, 4608:5120]
        hs = [area_q[:, 512 * i:512 * i + 512] for i in range(2)]
        ysb = [area_q[:, 1024 + 512 * i:1536 + 512 * i] for i in range(2)]
        rt = area_q[:, 2048:3072]
        rbias_sb = area_q[:, 4200:4236]
        key = area_q[:, 3072:3168].rearrange("p (t e) -> p t e", t=NT)
        val = area_q[:, 3168:3264].rearrange("p (t e) -> p t e", t=NT)
        okey = area_q[:, 3264:3264 + 2 * NT * (OVER + 1)].rearrange("p (k t b) -> p k t b", k=2, t=NT)
        pval = area_q[:, 3340:3346].rearrange("p (k t) -> p k t", k=2)
        assert 3264 + 2 * NT * (OVER + 1) <= 3340
        pairs = area_q[:, 3072:9216].rearrange("p (t k d) -> p t k d", t=NT, k=2)

        ss, rstd = small_cut(4), small_cut(4)
        qss, qrs = small_cut(NT, QK_HEADS), small_cut(NT, QK_HEADS)
        gates, absf = small_cut(NT, 16), small_cut(NT, 8)
        li, lf = small_cut(3, 8), small_cut(3, 8)
        bcum, btot, rrow = small_cut(3, 8), small_cut(3, 8), small_cut(3, 8)
        mstate, gcol, gall, gpick = small_cut(8), small_cut(8), small_cut(8), small_cut(8)
        expo = [small_cut(4, 8), area_m[:, 4952:4984].rearrange("p (a b) -> p a b", a=4)]
        dena = area_m[:, 4984:4992]
        den, nst, nout, mout = small_cut(4), small_cut(8), small_cut(8), small_cut(8)
        negm, lsum, rlsum = small_cut(8), small_cut(8), small_cut(8)
        wtop = small_cut(NT, 2)
        hss = small_cut(NT, 4)
        assert used[0] <= 444, used
        eid_i = sb("eid_i", [P, OVER + 1], I32)
        idx = [sb(f"idx{u}", [P, 1], U32) for u in range(2)]

        landed = [sem(f"weights_landed{i}") for i in range(RING)]
        S = {n: sem(n) for n in (
            "x_loaded", "keep_loaded", "early_loaded", "cond_loaded", "cond_silu", "cond_rep",
            "ada_done", "ada_copied", "ada_stored0", "ada_stored1", "cgain_loaded", "bias_row_loaded", "first_gain_loaded", "first_spread", "first_B", "cmod_loaded", "cmod_ready", "cmod_stored",
            "modAB_loaded", "modG_loaded", "squares", "h_ready", "trans_done", "trans_copied",
            "proj_done", "proj_copied_dve", "proj_copied_act", "small_loaded", "wge_loaded",
            "dve_step", "act_step", "qk_ready", "kv_stored", "gates_in", "gates_log", "lf_ready",
            "cum_done", "bt_done", "bt_copied_q", "bt_copied_k", "rrow_ready", "rows_done", "sums_done", "expo_ready",
            "wexp_ready", "wexp_done", "bs_done", "amat_ready", "amatT_done", "amatT_copied", "bnum_done",
            "kw_ready", "bupd_done", "combined", "cstate_ready", "state_loaded", "state_stored", "hm_squares", "hm_rooted", "qk_squares", "qk_rooted",
            "ogate_done", "bout_ready", "kdup_ready", "na_ctx_loaded", "na_v_loaded", "bias_loaded", "bias_ready",
            "pair_done", "qT_copied", "kT_copied", "scores_done", "max_ready", "prob_ready", "probT_done",
            "probT_copied", "pv_done", "heads_out", "outT_done", "outT_copied", "out_done", "x_mixed",
            "logits_done", "route_exp", "route_exped", "chosen", "ranks_done", "chosen_keys", 
            "over_ready",
            "pairs_loaded0", "pairs_loaded1", "pairs_loaded2", "pair_scaled", "x_moe",
            "y_ready", "y_stored", "gfin_loaded", "x_rest", "ctx_v", "wge_w")}

        def block_sems(tag, *more):
            return {n: sem(f"{tag}_{n}") for n in more + (
                "sel_ready", "tok_done", "tok_copied", "index_done", "index_ready", "xT_done", "xT_copied", "hid_done", "hidT_done",
                "upT_copied", "hidT_ready", "y_done", "y_copied", "scattered0")}

        M = block_sems("moe", "silu_done", "up_copied", "scattered1")
        OV = [block_sems(f"over{l}", "hs_ready") for l in range(2)]
        over_landed = [sem(f"over{l}_landed") for l in range(2)]

        ADA_STEPS = ((("in", 0), 2), (("in", 1), 2), (("in", 2), 2), (("in", 3), 2), (("in", 4), 2), (("in", 5), 2), ("turned", 2), ("summed", 1), ("scored", 1), (("stage", 0), 1), (("stage", 1), 1), (("stage", 2), 2))
        ADA_AT, ADA_GROUPS = {}, {}
        rest = [(0, c) for c in range(4, ADA_CHUNKS)] + [(1, c) for c in range(ADA_CHUNKS)]
        for _step, _n in ADA_STEPS:
            ADA_AT[_step], rest = rest[:_n], rest[_n:]
            ADA_GROUPS[_step] = [3 * l + c // 4 for l, c in ADA_AT[_step] if c % 4 == 3]
        assert not rest
        stream = [("ada", 0, c) for c in range(4)]
        for _step, _ in ADA_STEPS:
            if _step[0] == "in":
                stream.append(("in", 0, _step[1]))
            stream += [("ada",) + q for q in ADA_AT[_step]]
        for l in range(2):
            if l:
                stream += [("in", 1, c) for c in range(NA_CHUNKS)]
            stream += [("out", l, c) for c in range(OUT_CHUNKS)]
            stream += [("moe", l, c) for c in range(3 * EXPERTS)]
        NUM = {key: n for n, key in enumerate(stream)}
        IN_CHUNKS = (AB_CHUNKS, NA_CHUNKS)
        IN_W = (AB_W, NA_W)
        PROJ0 = (0, AB_CHUNKS * NT)

        def place(n):
            return n % RING

        def when(n):
            return 16 * (n // RING + 1)

        def freed(eng, n):
            kind, l, c = stream[n]
            if kind == "ada":
                eng.wait_ge(S["ada_done"], l * ADA_CHUNKS + c + 1)
            if kind == "in":
                eng.wait_ge(S["proj_done"], PROJ0[l] + NT * (c + 1))
            if kind == "out":
                eng.wait_ge(S["out_done"], (l + 1) * NT * OUT_CHUNKS)
            if kind == "moe":
                e, j = divmod(c, 3)
                eng.wait_ge(M["y_done"] if j == 2 else M["hid_done"], l * EXPERTS + e + 1)

        def stored(G):
            return 64 * ((G + 1) // 2)

        def spread_view(row):
            return row.rearrange("p (c j n) -> p j c n", c=2, j=4)

        def spread_banks(c, v):
            return psum[:, 4 * c + 2 * v:4 * c + 2 * v + 2, :].rearrange("p x (y c n) -> p (x y) c n", y=2, c=2)

        def wchunk(n, k):
            return ring[:, place(n), :].rearrange("p (k n) -> p k n", k=k)

        def expert_dram(l, e, j):
            one = (l, e) if isinstance(e, int) else (l, bass.ds(e, 1))
            if j == 2:
                v = a["moe_w2"][l].rearrange("e (p k) n -> e p (k n)", k=4)
                return v[e] if isinstance(e, int) else v[bass.ds(e, 1)].rearrange("e p n -> (e p) n")
            w = a["moe_w1" if j == 0 else "moe_w3"][l].rearrange("e (h p k) n -> e p h (k n)", h=2, k=4)
            return w[e] if isinstance(e, int) else w[bass.ds(e, 1)].rearrange("e p h n -> (e p) h n")

        def expert_dst(view, j):
            return view if j == 2 else view.rearrange("p (h n) -> p h n", h=2)

        STAGES = ((0, 0), (1, 2), (2, 1))
        NP = (A_HEADS // 2, C_HEADS // 2)
        NU = tuple(n * NT for n in NP)
        U0 = (0, NU[0])

        def unit(i):
            return i // NT, i % NT

        def keys_of(t):
            return (0, P) if t == 0 else (P, 4 * P)

        def scat(e, u, base):
            if isinstance(e, int):
                return 16 * ((e + base) // 2 + 1)
            return e * 8 + (8 * base - 8 * u + 16)

        block = ctx.enter_context(nc.Block())

        @block.sync
        def _(sp):
            def load(n, dst, src):
                if n >= RING:
                    freed(sp, n - RING)
                sp.dma_start(dst, src).then_inc(landed[place(n)], 16)

            matrix = {("ada", 0): a["ada_w"][0], ("ada", 1): a["ada_w"][1], ("in", 0): a["ab_w_in"][0],
                      ("in", 1): a["na_w_in"][0], ("out", 0): a["ab_w_out"][0], ("out", 1): a["na_w_out"][0]}

            def load_rows(kind, l, c):
                n = NUM[kind, l, c]
                src = matrix[kind, l].rearrange("(p k) n -> p k n" if kind == "ada" else "(k p) n -> p k n", p=P)
                w = min(512, src.shape[2] - 512 * c)
                load(n, wchunk(n, KT)[:, :, 0:w], src[:, :, 512 * c:512 * c + w])

            def load_experts(l):
                base = NUM["moe", l, 0]

                def one(e, u):
                    for j in range(3):
                        at = place(base + 3 * u + j)
                        dst = expert_dst(ring[:, at, :], j)
                        if isinstance(e, int) and e < 2:
                            freed(sp, base + 3 * e + j - RING)
                        else:
                            sp.wait_ge(M["y_done"] if j == 2 else M["hid_done"], e + (l * EXPERTS - 1))
                        sp.dma_start(dst, expert_dram(l, e, j)).then_inc(landed[at], 16)

                one(0, 0)
                one(1, 1)
                with sp.Fori(1, EXPERTS // 2) as i:
                    for u in range(2):
                        one(sp.snap(i * 2 + u), u)

            def load_overflow(l):
                sp.wait_ge(S["over_ready"], l + 1)
                n_over = sp.value_load(eid_i[0:1, OVER:OVER + 1], min_val=0, max_val=OVER)
                V = OV[l]
                with sp.If(n_over > 0):
                    sp.wait_ge(M["y_done"], (l + 1) * EXPERTS)

                    def one(b, first):
                        e = sp.value_load(eid_i[0:1, 0:1] if first else eid_i[0:1, bass.ds(b, 1)],
                                          min_val=0, max_val=EXPERTS - 1)
                        for j in range(3):
                            if not first:
                                sp.wait_ge(V["y_done"] if j == 2 else V["hid_done"], b)
                            sp.dma_start(expert_dst(ring[:, j, :], j), expert_dram(l, e, j)).then_inc(over_landed[l], 16)

                    one(0, True)
                    with sp.Fori(1, OVER) as b:
                        one(b, False)
                    sp.wait_ge(V["y_done"], OVER)

            sp.dma_start(condr[:, 0, :], a["c_ctx"].rearrange("(p k) -> p k", p=P)).then_inc(S["cond_loaded"], 16)
            sp.dma_start(condr[:, 1, :], a["c"][0].rearrange("(p k) -> p k", p=P)).then_inc(S["cond_loaded"], 16)
            for key in stream[:NUM["moe", 0, 0]]:
                if key == ("in", 0, 0):
                    sp.wait_ge(S["first_gain_loaded"], 16)
                load_rows(*key)
            load_experts(0)
            load_overflow(0)
            for n in range(NUM["in", 1, 0], NUM["moe", 1, 0]):
                if n == NUM["in", 1, 1]:
                    sp.wait_ge(S["pairs_loaded2"], 16)
                load_rows(*stream[n])
            load_experts(1)
            load_overflow(1)

        @block.tensor
        def _(pe):
            def ada(l, c):
                n = NUM["ada", l, c]
                if l == 0 and c == 0:
                    pe.wait_ge(S["cond_rep"], 1)
                pe.wait_ge(landed[place(n)], when(n))
                g = l * 3 + c // 4
                if c % 4 == 0 and g:
                    pe.wait_ge(S["ada_copied"], g)
                w = wchunk(n, KT)
                for k in range(KT):
                    for j in range(4):
                        mm = pe.matmul(banks[7][32 * j:32 * j + 32, 128 * (c % 4):128 * (c % 4) + 128],
                                       cond32[:, k, :], w[:, k, 128 * j:128 * j + 128],
                                       start=(k == 0), stop=(k == KT - 1 and not (l == 0 and c < 4)),
                                       skip_group_check=True)
                if l == 0 and c < 4:
                    if c == 0:
                        pe.wait_ge(S["bias_row_loaded"], 16)
                    for j in range(4):
                        mm = pe.matmul(banks[7][32 * j:32 * j + 32, 128 * c:128 * c + 128], ones[0:1, 0:32],
                                       bias_row[:, 512 * c + 128 * j:512 * c + 128 * j + 128],
                                       start=False, stop=True, skip_group_check=True)
                mm.then_inc(S["ada_done"], 1)

            def ada_step(which):
                for q in ADA_AT[which]:
                    ada(*q)

            def spread_first():
                pe.wait_ge(S["ada_copied"], 1)
                for c in range(2):
                    for v in range(2):
                        for j in range(4):
                            row = 32 * j + 16 * c
                            mm = pe.matmul(banks[4 * c + 2 * v + j // 2][:, 256 * (j % 2):256 * (j % 2) + 256],
                                           ident[:, row:row + 1].to_broadcast([P, P]),
                                           modsb[:, 0, 2 * v:2 * v + 2, :].rearrange("p c n -> p (c n)"),
                                           start=True, stop=True)
                    mm.then_inc(S["first_spread"], 1)

            def transpose_rows(idx, t):
                pe.wait_ge(S["h_ready"], NT * idx + t + 1)
                for half in range(2):
                    n = 2 * (NT * idx + t) + half
                    if n >= 2:
                        pe.wait_ge(S["trans_copied"], n - 1)
                    for k in range(4):
                        d0 = (4 * half + k) * P
                        mm = pe.transpose(banks[n % 2][:, k * P:k * P + P], h[:, t, d0:d0 + P], ident)
                    mm.then_inc(S["trans_done"], 1)

            def project(l):
                for c in range(IN_CHUNKS[l]):
                    n = NUM["in", l, c]
                    w = min(512, IN_W[l] - 512 * c)
                    pe.wait_ge(landed[place(n)], when(n))
                    for t in range(NT):
                        g = PROJ0[l] + NT * c + t
                        if c == 0:
                            pe.wait_ge(S["trans_copied"], 2 * (NT * 2 * l + t + 1))
                        if g >= 4:
                            pe.wait_ge(S["proj_copied_act" if g % 2 else "proj_copied_dve"], (g - 4) // 2 + 1)
                        for k in range(KT):
                            mm = pe.matmul(banks[2 + g % 4][:, 0:w], hT[:, k, t * P:t * P + P],
                                           wchunk(n, KT)[:, k, 0:w], start=(k == 0), stop=(k == KT - 1))
                        mm.then_inc(S["proj_done"], 1)
                    if l == 0:
                        ada_step(("in", c))

            def mlstm():
                for n in range(2 * NT):
                    t, side = n // 2, n % 2
                    if n == 0:
                        pe.wait_ge(S["proj_copied_dve"], AB_CHUNKS * NT // 2)
                        pe.wait_ge(S["proj_copied_act"], AB_CHUNKS * NT // 2)
                    if n >= 2:
                        pe.wait_ge(S["bt_copied_k" if side else "bt_copied_q"], t)
                    for hh in range(B_HEADS):
                        c0 = (BK if side else BQ) + hh * BD
                        mm = pe.transpose(banks[3 + side][:, hh * P:hh * P + P], qkv[0][:, t, c0:c0 + BD], ident)
                    mm.then_inc(S["bt_done"], 1)
                ada_step("turned")
                pe.wait_ge(S["lf_ready"], 1)
                pe.wait_ge(S["early_loaded"], 16)
                for s in range(3):
                    pe.matmul(banks[0][:, 16 * s:16 * s + 4], trif, lf[:, s, 0:4], start=True, stop=True)
                    pe.matmul(banks[0][:, 16 * s + 4:16 * s + 8], early[:, EARLY["trib"]], lf[:, s, 4:8],
                              start=True, stop=True)
                    mm = pe.matmul(banks[0][:, 16 * s + 8:16 * s + 16], ones, lf[:, s, :], start=True, stop=True)
                mm.then_inc(S["cum_done"], 1)
                ada_step("summed")
                def rows(s):
                    if s == 0:
                        pe.wait_ge(S["rrow_ready"], 1)
                    else:
                        pe.wait_ge(S["expo_ready"], s)
                    if s == 2:
                        pe.wait_ge(S["combined"], 2)
                        pe.wait_ge(S["cstate_ready"], 2)
                    for u in range(8):
                        mm = pe.matmul(banks[1 + u // 4][:, (u % 4) * P:(u % 4) * P + P],
                                       rrow[:, s, u:u + 1].to_broadcast([P, P]), ident, start=True, stop=True)
                    mm.then_inc(S["rows_done"], 1)

                def state_products(s, d):
                    for hh in range(B_HEADS):
                        pe.matmul(banks[6][:, hh * P:hh * P + P], bqT[:, hh, tok[d]], Cst[:, 4 * d + hh, :],
                                  start=True, stop=True)

                def turn_weights(v, d):
                    pe.wait_ge(S["amat_ready"], v + 1)
                    if v:
                        pe.wait_ge(S["amatT_copied"], v)
                    for hh in range(B_HEADS):
                        mm = pe.transpose(banks[4][:, hh * P:hh * P + P], amat[d][:, hh, :], ident)
                    mm.then_inc(S["amatT_done"], 1)

                def number_products(v, d):
                    pe.wait_ge(S["amatT_copied"], v + 1)
                    for hh in range(B_HEADS):
                        mm = pe.matmul(banks[5][:, hh * P:hh * P + P], amatT[:, hh, :],
                                       qkv[0][:, STAGES[s][d], BV + hh * BD:BV + hh * BD + BD], start=True, stop=True)
                    mm.then_inc(S["bnum_done"], 1)

                rows(0)
                for s in range(3):
                    tok = [slice(t * P, t * P + P) for t in STAGES[s]]
                    for d in range(2):
                        if s == 0 and d == 0:
                            pe.wait_ge(S["bt_copied_q"], NT)
                            pe.wait_ge(S["bt_copied_k"], NT)
                        if s:
                            pe.wait_ge(S["cstate_ready"], 2 * (s - 1) + d + 1)
                        for hh in range(B_HEADS):
                            mm = pe.matmul(banks[(3, 0)[d]][:, hh * P:hh * P + P], bqT[:, hh, tok[d]],
                                           bkT[:, hh, tok[d]], start=True, stop=True)
                        mm.then_inc(S["bs_done"], 1)
                    if s < 2:
                        rows(s + 1)
                    if s == 0:
                        ada_step("scored")
                    v = 2 * s
                    turn_weights(v, 0)
                    if v:
                        pe.wait_ge(S["combined"], v)
                    if s == 1:
                        pe.wait_ge(S["state_loaded"], 48)
                    if s:
                        state_products(s, 0)
                    number_products(v, 0)
                    turn_weights(v + 1, 1)
                    if s < 2:
                        for d in range(2):
                            pe.wait_ge(S["kw_ready"], v + d + 1)
                            for hh in range(B_HEADS):
                                mm = pe.matmul(banks[(3, 0)[d]][:, hh * P:hh * P + P], kw[d][:, hh, :],
                                               qkv[0][:, STAGES[s][d], BV + hh * BD:BV + hh * BD + BD],
                                               start=True, stop=True)
                            mm.then_inc(S["bupd_done"], 1)
                        pe.wait_ge(S["expo_ready"], s + 2)
                    for d in range(2):
                        for hh in range(B_HEADS):
                            if s:
                                mm = pe.matmul(banks[1][:, 4 * d + hh:4 * d + hh + 1], bqT[:, hh, tok[d]],
                                               nst[:, 4 * d + hh:4 * d + hh + 1], start=True, stop=True)
                            if s < 2:
                                mm = pe.matmul(banks[2][:, 4 * d + hh:4 * d + hh + 1], kw[d][:, hh, :], ones[:, 0:1],
                                               start=True, stop=True)
                    mm.then_inc(S["sums_done"], 1)
                    pe.wait_ge(S["combined"], v + 1)
                    if s:
                        state_products(s, 1)
                    number_products(v + 1, 1)
                    ada_step(("stage", s))

            def turn_queries(l, j):
                if l == 0 and j == 0:
                    pe.wait_ge(S["kdup_ready"], 1)
                    pe.wait_ge(S["ctx_v"], 16)
                if l == 1 and j == 0:
                    for name in ("proj_copied_dve", "proj_copied_act"):
                        pe.wait_ge(S[name], (PROJ0[1] + NA_CHUNKS * NT) // 2)
                    pe.wait_ge(S["na_ctx_loaded"], 16)
                    pe.wait_ge(S["bias_ready"], 1)
                g = (0, NP[0])[l] + j
                if g:
                    pe.wait_ge(S["kT_copied"], g)
                else:
                    pe.wait_ge(S["ada_copied"], 6)
                for t in range(NT):
                    mm = pe.transpose(banks[7][:, t * P:t * P + P], qkv[l][:, t, 2 * HD * j:2 * HD * j + 2 * HD], ident)
                mm.then_inc(S["pair_done"], 1)

            def turn_keys(l, j):
                g = (0, NP[0])[l] + j
                pe.wait_ge(S["qT_copied"], g + 1)
                for s in range(4):
                    if l == 0:
                        src = kdup[:, j // 2, s, :, :]
                    elif s == 1:
                        src = na_k[:, 2 * HD * j:2 * HD * j + 2 * HD]
                    else:
                        src = qkv[1][:, (0, None, 1, 2)[s], D + 2 * HD * j:D + 2 * HD * j + 2 * HD]
                    mm = pe.transpose(banks[7][:, s * P:s * P + P], src, ident)
                mm.then_inc(S["pair_done"], 1)

            def scores(l, i):
                j, t = unit(i)
                U = U0[l] + i
                k0, k1 = keys_of(t)
                g = (0, NP[0])[l] + j
                pe.wait_ge(S["qT_copied"], g + 1)
                pe.wait_ge(S["kT_copied"], g + 1)
                if U >= 2:
                    pe.wait_ge(S["prob_ready"], U - 1)
                biased = l == 1 and t > 0
                for hh in range(2):
                    rows = slice(64 * hh, 64 * hh + 64)
                    mm = pe.matmul(psum[:, 2 * (U % 2) + hh, 0:k1 - k0], qT[l][rows, g % 2, t * P:t * P + P],
                                   kT[l][rows, g % 2, k0:k1], start=True, stop=not biased)
                if biased:
                    r0 = 4 - 2 * t
                    for hh in range(2):
                        mm = pe.matmul(psum[:, 2 * (U % 2) + hh, P:3 * P], flip, bias_na[:, 2 * j + hh, r0:r0 + ROWS, :],
                                       start=False, stop=True)
                mm.then_inc(S["scores_done"], 1)

            def turn_probs(l, i):
                j, t = unit(i)
                U = U0[l] + i
                pe.wait_ge(S["prob_ready"], U + 1)
                if U >= 1:
                    pe.wait_ge(S["probT_copied"], U)
                k0, k1 = keys_of(t)
                for hh in range(2):
                    for s in range((k1 - k0) // P):
                        mm = pe.transpose(banks[4 + hh][:, s * P:s * P + P], prob[:, U % 2, hh, s * P:s * P + P], ident)
                mm.then_inc(S["probT_done"], 1)

            def values(l, i):
                j, t = unit(i)
                U = U0[l] + i
                pe.wait_ge(S["probT_copied"], U + 1)
                if U >= 1:
                    pe.wait_ge(S["heads_out"], U)
                if l == 1 and i == 1:
                    pe.wait_ge(S["na_v_loaded"], 16)
                for hh in range(2):
                    c0 = (AV + (j // 2) * HD) if l == 0 else 2 * D + (2 * j + hh) * HD
                    vs = [qkv[l][:, tt, c0:c0 + HD] for tt in range(NT)]
                    if l == 0:
                        cached = ctx_kv[:, 1, (j // 2) * HD:(j // 2) * HD + HD]
                    else:
                        cached = na_v[:, (2 * j + hh) * HD:(2 * j + hh) * HD + HD]
                    vs = vs[0:1] if t == 0 else [cached] + vs[1:]
                    for s, v in enumerate(vs):
                        mm = pe.matmul(banks[6][:, HD * hh:HD * hh + HD], probT[U % 2][:, hh, s * P:s * P + P], v,
                                       start=(s == 0), stop=(s == len(vs) - 1))
                mm.then_inc(S["pv_done"], 1)

            def attention(l):
                turn_queries(l, 0)
                turn_keys(l, 0)
                for i in range(NU[l] + 2):
                    if i % NT == 0 and i // NT + 1 < NP[l]:
                        turn_queries(l, i // NT + 1)
                    if i % NT == 1 and i // NT + 1 < NP[l]:
                        turn_keys(l, i // NT + 1)
                    if i < NU[l]:
                        scores(l, i)
                    if 1 <= i <= NU[l]:
                        turn_probs(l, i - 1)
                    if i >= 2:
                        values(l, i - 2)

            def project_out(l):
                for t in range(NT):
                    for half in range(2):
                        n = 2 * (NT * l + t) + half
                        if n % (2 * NT) == 0:
                            pe.wait_ge(S["heads_out"], U0[l] + NU[l])
                            if l == 0:
                                pe.wait_ge(S["bout_ready"], NT)
                        if n >= 2:
                            pe.wait_ge(S["outT_copied"], n - 1)
                        c0 = BQ if (l == 0 and half == 1) else 512 * half
                        for k in range(4):
                            mm = pe.transpose(banks[n % 2][:, k * P:k * P + P],
                                              qkv[l][:, t, c0 + k * P:c0 + k * P + P], ident)
                        mm.then_inc(S["outT_done"], 1)
                for t in range(NT):
                    if t == NT - 1:
                        transpose_rows(2 * l + 1, 0)
                        logits(l, 0)
                    pe.wait_ge(S["outT_copied"], 2 * (NT * l + t + 1))
                    for c in range(OUT_CHUNKS):
                        n = NUM["out", l, c]
                        pe.wait_ge(landed[place(n)], when(n))
                        g = l * NT * OUT_CHUNKS + t * OUT_CHUNKS + c
                        if g >= 2:
                            pe.wait_ge(S["x_mixed"], g - 1)
                        for k in range(KT):
                            mm = pe.matmul(banks[2 + g % 2][:, :], hT[:, k, t * P:t * P + P],
                                           wchunk(n, KT)[:, k, :], start=(k == 0), stop=(k == KT - 1))
                        mm.then_inc(S["out_done"], 1)

            def logits(l, t):
                if t == 0:
                    pe.wait_ge(S["wge_w"], 32 * (l + 1))
                pe.wait_ge(S["trans_copied"], 2 * (NT * (2 * l + 1) + t + 1))
                for k in range(KT):
                    mm = pe.matmul(banks[6][:, 36 * t:36 * t + 36], hT[:, k, t * P:t * P + P], wge[:, k, :],
                                   start=(k == 0), stop=(k == KT - 1))
                if t == NT - 1:
                    mm.then_inc(S["logits_done"], 1)

            def ranks(l):
                pe.wait_ge(S["chosen"], l + 1)
                chosen = rt[:, 0:96].rearrange("p (t e) -> p t e", t=NT)
                pe.matmul(banks[2][:, 0:32], trif, chosen[:, 0, :], start=True, stop=True)
                for s in range(NT):
                    mm = pe.matmul(banks[2][:, 32 * (s + 1):32 * (NT + 1)], ones,
                                   chosen[:, s, :].unsqueeze(1).to_broadcast([P, NT - s, 32]),
                                   start=(s == 0), stop=(s == NT - 1), skip_group_check=True)
                    if s == 0:
                        pe.matmul(banks[2][:, 32:32 * NT], trif, chosen[:, 1:NT, :], start=False, stop=False,
                                  skip_group_check=True)
                mm.then_inc(S["ranks_done"], 1)

            def token_products(picks):
                for n, (pick, t) in enumerate(picks):
                    for half in range(2):
                        mm = pe.matmul(banks[0][64 * half:64 * half + 64, :], pick[:, 0:BLOCK],
                                       h[:, t, 512 * half:512 * half + 512], start=(n == 0), stop=(n == len(picks) - 1))
                return mm

            def token_turns():
                for k in range(4):
                    mm = pe.transpose(banks[1][:, k * P:k * P + P], tok[:, k:512:4], ident)
                return mm

            def index_products(picks):
                for n, (pick, value) in enumerate(picks):
                    mm = pe.matmul(banks[5][:, 0:1], pick, value, start=(n == 0), stop=(n == len(picks) - 1))
                return mm

            def hidden_products(u, w1, w3):
                for k in range(KT):
                    lhsT = xT[u][:, k % 4, 64 * (k // 4):64 * (k // 4) + 64]
                    pe.matmul(banks[2 + u][0:64, :], lhsT, w1[:, k, :], start=(k == 0), stop=(k == KT - 1))
                    mm = pe.matmul(banks[2 + u][64:128, :], lhsT, w3[:, k, :], start=(k == 0), stop=(k == KT - 1))
                return mm

            def hidden_turns(u):
                for k in range(4):
                    mm = pe.transpose(banks[4][:, k * P:k * P + P], hs[u][:, k:512:4], ident)
                return mm

            def down_products(u, w2):
                for k in range(4):
                    for j in range(2):
                        mm = pe.matmul(banks[6 + u][64 * j:64 * j + 64, :], hidT[u][:, k, :],
                                       w2[:, k, 512 * j:512 * j + 512], start=(k == 0), stop=(k == 3))
                return mm

            def tokens(e, u, base):
                pe.wait_ge(M["sel_ready"], e + (base + 1))
                if not (isinstance(e, int) and e + base < 1):
                    pe.wait_ge(M["tok_copied"], e + base)
                token_products([(sel[u][:, t, :], t) for t in range(NT)]).then_inc(M["tok_done"], 1)

            def turn_tokens(e, u, base):
                if not (isinstance(e, int) and e + base < 1):
                    pe.wait_ge(M["index_ready"], e + base)
                column = [val[:, t, e:e + 1] if isinstance(e, int) else val[:, t, bass.ds(e, 1)] for t in range(NT)]
                index_products([(sel[u][:, t, :], column[t]) for t in range(NT)]).then_inc(M["index_done"], 1)
                pe.wait_ge(M["tok_copied"], e + (base + 1))
                if not (isinstance(e, int) and e + base < 1):
                    pe.wait_ge(M["xT_copied"], e + base)
                token_turns().then_inc(M["xT_done"], 1)

            def hidden(e, u, base, w1, w3):
                pe.wait_ge(M["xT_copied"], e + (base + 1))
                if not (isinstance(e, int) and e + base < 2):
                    pe.wait_ge(M["silu_done"], e + (base - 1))
                    pe.wait_ge(M["up_copied"], e + (base - 1))
                hidden_products(u, w1, w3).then_inc(M["hid_done"], 1)

            def turn_hidden(e, u, base):
                pe.wait_ge(M["silu_done"], e + (base + 1))
                pe.wait_ge(M["up_copied"], e + (base + 1))
                if not (isinstance(e, int) and e + base < 1):
                    pe.wait_ge(M["hidT_ready"], e + base)
                hidden_turns(u).then_inc(M["hidT_done"], 1)

            def down(e, u, base, w2):
                pe.wait_ge(M["hidT_ready"], e + (base + 1))
                if not (isinstance(e, int) and e + base < 2):
                    pe.wait_ge(M["y_copied"], e + (base - 1))
                down_products(u, w2).then_inc(M["y_done"], 1)

            def experts(l):
                start = NUM["moe", l, 0]
                base = l * EXPERTS

                def wait_chunk(e, u, j):
                    n = start + 3 * u + j
                    rounds = (e - u) * 8 if isinstance(e, int) else (e * 8 - 8 * u)
                    pe.wait_ge(landed[place(n)], rounds + when(n))

                def one(e, u, last):
                    ws = [wchunk(start + 3 * u + j, 4 if j == 2 else KT) for j in range(3)]
                    wait_chunk(e, u, 0)
                    wait_chunk(e, u, 1)
                    hidden(e, u, base, ws[0], ws[1])
                    if not last:
                        tokens(e + 1, 1 - u, base)
                    turn_hidden(e, u, base)
                    if last:
                        pe.wait_ge(M["index_ready"], e + (base + 1))
                    else:
                        turn_tokens(e + 1, 1 - u, base)
                    wait_chunk(e, u, 2)
                    down(e, u, base, ws[2])

                tokens(0, 0, base)
                turn_tokens(0, 0, base)
                one(0, 0, False)
                one(1, 1, False)
                with pe.Fori(1, EXPERTS // 2 - 1) as i:
                    for u in range(2):
                        one(pe.snap(i * 2 + u), u, False)
                one(EXPERTS - 2, 0, False)
                one(EXPERTS - 1, 1, True)

            def overflow(l):
                V = OV[l]
                pe.wait_ge(S["over_ready"], l + 1)
                n_over = pe.value_load(eid_i[0:1, OVER:OVER + 1], min_val=0, max_val=OVER)
                with pe.If(n_over > 0):
                    with pe.Fori(0, OVER) as b:
                        pe.wait_ge(V["sel_ready"], b + 1)
                        token_products([(sel[k][:, t, :], t) for k in range(2) for t in range(NT)])\
                            .then_inc(V["tok_done"], 1)
                        index_products([(sel[k][:, t, :], pval[:, k, t:t + 1]) for k in range(2) for t in range(NT)])\
                            .then_inc(V["index_done"], 1)
                        pe.wait_ge(V["tok_copied"], b + 1)
                        token_turns().then_inc(V["xT_done"], 1)
                        pe.wait_ge(over_landed[l], b * 48 + 48)
                        pe.wait_ge(V["xT_copied"], b + 1)
                        hidden_products(0, *(ring[:, j, :].rearrange("p (k n) -> p k n", k=KT) for j in range(2)))\
                            .then_inc(V["hid_done"], 1)
                        pe.wait_ge(V["index_ready"], b + 1)
                        pe.wait_ge(V["hs_ready"], b * 2 + 2)
                        hidden_turns(0).then_inc(V["hidT_done"], 1)
                        pe.wait_ge(V["hidT_ready"], b + 1)
                        down_products(0, ring[:, 2, :].rearrange("p (k n) -> p k n", k=4)).then_inc(V["y_done"], 1)

            pe.wait_ge(S["keep_loaded"], 16)
            for c in range(4):
                ada(0, c)
            spread_first()
            for l in range(2):
                for t in range(NT):
                    transpose_rows(2 * l, t)
                project(l)
                if l == 0:
                    mlstm()
                attention(l)
                project_out(l)
                for t in range(1, NT):
                    transpose_rows(2 * l + 1, t)
                    logits(l, t)
                ranks(l)
                experts(l)
                overflow(l)

        @block.scalar
        def _(act):
            count = {}

            def step(ins, name, hold=False):
                ins.then_inc(S[name], 1)
                count[name] = count.get(name, 0) + 1
                if hold:
                    act.wait_ge(S[name], count[name])

            act.wait_ge(S["cond_loaded"], 32)
            step(act.activation(condr[:, :, :], condr[:, :, :], ACT.Silu), "cond_silu")

            def ada_copy(g):
                act.wait_ge(S["ada_done"], 4 * (g + 1))
                if g >= 3:
                    act.wait_ge(S[f"ada_stored{g % 2}"], stored(g - 2))
                step(act.copy(modsb[:, g % 2, :, :].rearrange("p c n -> p (c n)"), banks[7][:, :]), "ada_copied")

            def ada_copies(which):
                for g in ADA_GROUPS[which]:
                    ada_copy(g)

            def root(ap, n, name):
                step(act.activation(ap, ap, ACT.Sqrt, scale=1.0 / n, bias=keep[:, KEEP["eps"]]), name)

            def squares(t):
                step(act.activation(h[:, t, :], x[:, t, :], ACT.Square, accum_out=ss[:, t:t + 1]), "act_step",
                     hold=True)
                root(ss[:, t:t + 1], D, "squares")

            def copy_transposed(idx, t):
                for half in range(2):
                    n = 2 * (NT * idx + t) + half
                    act.wait_ge(S["trans_done"], n + 1)
                    step(act.copy(hT[:, 4 * half:4 * half + 4, t * P:t * P + P],
                                  banks[n % 2][:, :].rearrange("p (k n) -> p k n", k=4)), "trans_copied")

            def copy_projected(l):
                for g in range(PROJ0[l], PROJ0[l] + IN_CHUNKS[l] * NT):
                    if g % 2 == 0:
                        continue
                    c, t = divmod(g - PROJ0[l], NT)
                    w = min(512, IN_W[l] - 512 * c)
                    act.wait_ge(S["proj_done"], g + 1)
                    step(act.copy(qkv[l][:, t, 512 * c:512 * c + w], banks[2 + g % 4][:, 0:w]), "proj_copied_act")
                    if l == 0 and g == 2 * NT + 1:
                        act.wait_ge(S["qk_squares"], 1)
                        root(qss[:, :, :], HD, "qk_rooted")
                    if l == 0 and (g + 2) // NT > c:
                        ada_copies(("in", c))

            def mlstm():
                for t in range(NT):
                    act.wait_ge(S["bt_done"], 2 * t + 1)
                    step(act.copy(bqT[:, :, t * P:t * P + P], banks[3][:, :].rearrange("p (u s) -> p u s", u=4)),
                         "bt_copied_q")
                act.wait_ge(S["gates_in"], 1)
                step(act.activation(absf[:, :, :], absf[:, :, :], ACT.Exp, scale=-1.0), "act_step", hold=True)
                step(act.activation(absf[:, :, :], absf[:, :, :], ACT.Ln, bias=1.0), "gates_log")
                def exponents(s):
                    act.wait_ge(S["expo_ready"], s + 1)
                    step(act.activation(expo[s % 2], expo[s % 2], ACT.Exp), "act_step")
                    act.wait_ge(S["wexp_ready"], s + 1)
                    step(act.activation(wexp[s % 2], wexp[s % 2], ACT.Exp), "wexp_done")

                ada_copies("turned")
                exponents(0)
                ada_copies("summed")
                ada_copies("scored")
                for s in range(3):
                    for d in range(2):
                        v = 2 * s + d
                        act.wait_ge(S["amatT_done"], v + 1)
                        if v:
                            act.wait_ge(S["bnum_done"], v)
                        step(act.copy(amatT[:, :, :].rearrange("p u s -> p (u s)"), banks[4][:, :]), "amatT_copied")
                    if s < 2:
                        exponents(s + 1)
                    ada_copies(("stage", s))
                for t in range(NT):
                    step(act.activation(qkv[0][:, t, BO:BO + 512], qkv[0][:, t, BO:BO + 512], ACT.Sigmoid),
                         "ogate_done")

            def attention(l):
                if l == 0:
                    act.wait_ge(S["state_stored"], 48)

                def copy_queries(j):
                    g = (0, NP[0])[l] + j
                    act.wait_ge(S["pair_done"], 2 * g + 1)
                    if j >= 2:
                        act.wait_ge(S["scores_done"], U0[l] + NT * (j - 1))
                    step(act.mul(qT[l][:, g % 2, :], banks[7][:, 0:TOKENS], HD ** -0.5), "qT_copied")

                copy_queries(0)
                for i in range(NU[l] + 1):
                    if l == 0 and i == 6:
                        act.wait_ge(S["hm_squares"], 1)
                        root(hss[:, :, :], BD, "hm_rooted")
                    if i >= 1:
                        U = U0[l] + i - 1
                        t = unit(i - 1)[1]
                        k0, k1 = keys_of(t)
                        act.wait_ge(S["probT_done"], U + 1)
                        if U >= 2:
                            act.wait_ge(S["pv_done"], U - 1)
                        step(act.copy(probT[U % 2][:, :, 0:k1 - k0], psum[:, 4:6, 0:k1 - k0]), "probT_copied")
                    if i < NU[l]:
                        j, t = unit(i)
                        U = U0[l] + i
                        act.wait_ge(S["max_ready"], U + 1)
                        if U >= 2:
                            act.wait_ge(S["probT_done"], U - 1)
                        k0, k1 = keys_of(t)
                        for hh in range(2):
                            col = 2 * (U % 4) + hh
                            ins = act.activation(prob[:, U % 2, hh, 0:k1 - k0], psum[:, 2 * (U % 2) + hh, 0:k1 - k0],
                                                 ACT.Exp, bias=negm[:, col:col + 1], accum_out=lsum[:, col:col + 1])
                        step(ins, "prob_ready")
                    if i % NT == 0 and i // NT + 1 < NP[l]:
                        copy_queries(i // NT + 1)

            def copy_out_transposed(l):
                for t in range(NT):
                    for half in range(2):
                        n = 2 * (NT * l + t) + half
                        act.wait_ge(S["outT_done"], n + 1)
                        step(act.copy(hT[:, 4 * half:4 * half + 4, t * P:t * P + P],
                                      banks[n % 2][:, :].rearrange("p (k n) -> p k n", k=4)), "outT_copied")

            def route(l):
                act.wait_ge(S["route_exp"], 2 * l + 1)
                g4 = rt[:, 96:108]
                step(act.activation(g4, g4, ACT.Exp), "route_exped")
                act.wait_ge(S["route_exp"], 2 * l + 2)
                d3 = rt[:, 108:111]
                step(act.activation(d3, d3, ACT.Exp), "route_exped")

            def copy_tokens(e, base):
                act.wait_ge(M["tok_done"], e + (base + 1))
                if not (isinstance(e, int) and e + base < 1):
                    act.wait_ge(M["xT_done"], e + base)
                act.copy(tok, banks[0][:, :]).then_inc(M["tok_copied"], 1)

            def one(e, u, base, last=False):
                def old(name):
                    if not (isinstance(e, int) and e + base < 2):
                        act.wait_ge(M[name], e + (base - 1))

                act.wait_ge(M["hid_done"], e + (base + 1))
                old("hidT_done")
                act.activation(hs[u][0:64, :], banks[2 + u][0:64, :], ACT.Silu).then_inc(M["silu_done"], 1)
                if not last:
                    copy_tokens(e + 1, base)
                act.wait_ge(M["hidT_done"], e + (base + 1))
                old("hidT_ready")
                act.copy(upT[u][:, :, :], banks[4][:, :].rearrange("p (k n) -> p k n", k=4)[:, :, 64:128])\
                    .then_inc(M["upT_copied"], 1)
                act.wait_ge(M["y_done"], e + (base + 1))
                if not (isinstance(e, int) and e + base < 2):
                    act.wait_ge(M[f"scattered{u}"], scat(e, u, base) - 16)
                act.copy(ysb[u], banks[6 + u][:, :]).then_inc(M["y_copied"], 1)

            def one_over(V, b):
                act.wait_ge(V["tok_done"], b + 1)
                act.copy(tok, banks[0][:, :]).then_inc(V["tok_copied"], 1)
                act.wait_ge(V["hid_done"], b + 1)
                act.activation(hs[0][0:64, :], banks[2][0:64, :], ACT.Silu).then_inc(V["hs_ready"], 1)
                act.wait_ge(V["hidT_done"], b + 1)
                act.copy(upT[0][:, :, :], banks[4][:, :].rearrange("p (k n) -> p k n", k=4)[:, :, 64:128])\
                    .then_inc(V["upT_copied"], 1)
                act.wait_ge(V["y_done"], b + 1)
                act.copy(ysb[0], banks[6][:, :]).then_inc(V["y_copied"], 1)

            def experts(l):
                base = l * EXPERTS
                copy_tokens(0, base)
                one(0, 0, base)
                one(1, 1, base)
                with act.Fori(1, EXPERTS // 2 - 1) as i:
                    for u in range(2):
                        one(act.snap(i * 2 + u), u, base)
                one(EXPERTS - 2, 0, base)
                one(EXPERTS - 1, 1, base, last=True)
                act.wait_ge(S["over_ready"], l + 1)
                n_over = act.value_load(eid_i[0:1, OVER:OVER + 1], min_val=0, max_val=OVER)
                with act.If(n_over > 0):
                    act.wait_ge(M["scattered0"], 16 * (l + 1) * EXPERTS // 2)
                    with act.Fori(0, OVER) as b:
                        one_over(OV[l], b)

            def scale_pairs(l, t):
                act.wait_ge(S[f"pairs_loaded{t}"], 16 * (l + 1))
                step(act.activation(pairs[:, t, 0, :], pairs[:, t, 0, :], ACT.Copy, scale=wtop[:, t, 0:1]),
                     "pair_scaled")

            def finish_layer(l):
                scale_pairs(l, 0)
                for t in range(NT):
                    if t + 1 < NT:
                        scale_pairs(l, t + 1)
                    act.wait_ge(S["x_moe"], NT * l + t + 1)
                    squares(t)

            for t in range(NT):
                act.wait_ge(S["x_loaded" if t == 0 else "x_rest"], 16)
                squares(t)
            ada_copy(0)
            for c in range(2):
                act.wait_ge(S["first_spread"], c + 1)
                step(act.copy(spread_view(modB[:, c, :]), spread_banks(c, 0)), "first_B")
            for l in range(2):
                for t in range(NT):
                    copy_transposed(2 * l, t)
                copy_projected(l)
                if l == 0:
                    mlstm()
                attention(l)
                copy_out_transposed(l)
                for t in range(NT):
                    act.wait_ge(S["x_mixed"], 2 * (NT * l + t + 1))
                    squares(t)
                    if t:
                        copy_transposed(2 * l + 1, t - 1)
                copy_transposed(2 * l + 1, NT - 1)
                route(l)
                experts(l)
                finish_layer(l)

        @block.vector
        def _(v):
            count = {}

            def do(ins, name="dve_step"):
                ins.then_inc(S[name], 1)
                count[name] = count.get(name, 0) + 1
                v.wait_ge(S[name], count[name])

            def tt(out, in0, in1, op, name="dve_step"):
                do(v.tensor_tensor(out, in0, in1, op), name)

            def ts(out, in0, s1, s2, op0, op1=None, name="dve_step"):
                do(v.tensor_scalar(out, in0, s1, s2, op0, op1) if op1 is not None else
                   v.tensor_scalar(out, in0, s1, s2, op0), name)

            def stt(out, in0, s, in1, op0, op1, name="dve_step"):
                do(v.scalar_tensor_tensor(out=out, in0=in0, scalar=s, in1=in1, op0=op0, op1=op1), name)

            def red(out, in_, op, name="dve_step"):
                do(v.tensor_reduce(out, in_, AX, op), name)

            def cp(out, in_, name="dve_step"):
                do(v.tensor_copy(out, in_), name)

            def last(ap, n):
                return ap.unsqueeze(len(ap.shape)).to_broadcast(list(ap.shape) + [n])

            def lead(ap, n):
                return ap.unsqueeze(1).to_broadcast([ap.shape[0], n] + list(ap.shape[1:]))

            v.wait_ge(S["cond_silu"], 1)
            for c in range(2):
                cp(cond32[:, :, 16 * c:16 * c + 16], last(condr[:, c, :], 16), "dve_step")
            do(v.memset(mstate[:, :], 0.0), "cond_rep")

            def modulation(G):
                l, g = divmod(G, 3)
                if G == 1:
                    v.wait_ge(S["cgain_loaded"], 96)
                v.wait_ge(S["cmod_loaded"], 32 * G)
                m = cmod[:, G % 2, :, :, :]
                for c in range(2):
                    tt(m[:, c, :, :], m[:, c, :, :], cada[:, l, 2 * g:2 * g + 2, :], ALU.add,
                       "cmod_ready" if (g == 1 and c == 1) else "dve_step")
                if g != 1:
                    at, gain = (1, 0) if g == 0 else (0, 1)
                    stt(m[:, :, at, :], m[:, :, at, :], 1.0, lead(cgain[:, l, gain, :], 2), ALU.add, ALU.mult,
                        "cmod_ready")

            def first_modulation():
                v.wait_ge(S["first_gain_loaded"], 16)
                for c in range(2):
                    v.wait_ge(S["first_spread"], c + 1)
                    for j in range(4):
                        stt(spread_view(modA[:, c, :])[:, j], spread_banks(c, 1)[:, j], 1.0,
                            spread_view(first_gain)[:, j], ALU.add, ALU.mult)
                v.wait_ge(S["first_B"], 2)

            def normed(idx, t):
                v.wait_ge(S["squares"], NT * idx + t + 1)
                do(v.reciprocal(rstd[:, t:t + 1], ss[:, t:t + 1]))
                if idx == 2 * 2:
                    if t == 0:
                        v.wait_ge(S["gfin_loaded"], 16)
                    stt(h[:, t, :], x[:, t, :], rstd[:, t:t + 1], modA[:, 0, :], ALU.mult, ALU.mult, "y_ready")
                    return
                if t == 0 and idx:
                    v.wait_ge(S["modAB_loaded"], 32 * idx)
                c = 0 if t == 0 else 1
                stt(h[:, t, :], x[:, t, :], rstd[:, t:t + 1], modA[:, c, :], ALU.mult, ALU.mult)
                tt(h[:, t, :], h[:, t, :], modB[:, c, :], ALU.add, "h_ready")

            def copy_projected(l):
                for g in range(PROJ0[l], PROJ0[l] + IN_CHUNKS[l] * NT):
                    if g % 2:
                        continue
                    c, t = divmod(g - PROJ0[l], NT)
                    w = min(512, IN_W[l] - 512 * c)
                    v.wait_ge(S["proj_done"], g + 1)
                    cp(qkv[l][:, t, 512 * c:512 * c + w], banks[2 + g % 4][:, 0:w], "proj_copied_dve")
                    if l == 0 and g == 2 * NT:
                        head_squares()
                    if l == 0 and g == 2 * NT + 2:
                        head_norms()
                    if l == 0 and (c, t) in ((3, 1), (5, 1)):
                        modulation(c // 2)
                    if l == 1 and g == PROJ0[1] + (NA_CHUNKS - 2) * NT:
                        window_bias()

            def gate_logs():
                v.wait_ge(S["proj_copied_act"], AB_CHUNKS * NT // 2)
                v.wait_ge(S["small_loaded"], 16 * 6)
                tt(gates[:, :, :], qkv[0][:, :, BG:BG + 16], lead(gbias, NT), ALU.add)
                f = gates[:, :, :].rearrange("p t (d g h) -> p t d g h", d=2, g=2)
                ab = absf[:, :, :].rearrange("p t (d h) -> p t d h", d=2)
                for d in range(2):
                    stt(ab[:, :, d, :], f[:, :, d, 1, :], -1.0, f[:, :, d, 1, :], ALU.mult, ALU.max,
                        "dve_step" if d == 0 else "gates_in")
                copy_b_keys()
                v.wait_ge(S["gates_log"], 1)
                for s in range(3):
                    for d in range(2):
                        t = STAGES[s][d]
                        cols = slice(4 * d, 4 * d + 4)
                        cp(li[:, s, cols], f[:, t, d, 0, :])
                        stt(lf[:, s, cols], f[:, t, d, 1, :], 0.0, ab[:, t, d, :], ALU.min, ALU.subtract,
                            "dve_step" if 2 * s + d < 5 else "lf_ready")

            def head_squares():
                v.wait_ge(S["proj_copied_act"], NT)
                scratch = area_h[:, 0:640].rearrange("p (u s) -> p u s", u=QK_HEADS)
                for t in range(NT):
                    z = qkv[0][:, t, 0:AV].rearrange("p (u s) -> p u s", u=QK_HEADS)
                    tt(scratch, z, z, ALU.mult)
                    red(qss[:, t, :], scratch, ALU.add, "dve_step" if t < NT - 1 else "qk_squares")

            def head_norms():
                v.wait_ge(S["early_loaded"], 16)
                v.wait_ge(S["small_loaded"], 16 * 6)
                scratch = area_h[:, 0:640].rearrange("p (u s) -> p u s", u=QK_HEADS)
                v.wait_ge(S["qk_rooted"], 1)
                do(v.reciprocal(qrs[:, :, :], qss[:, :, :]))
                for t in range(NT):
                    z = qkv[0][:, t, 0:AV].rearrange("p (u s) -> p u s", u=QK_HEADS)
                    tt(z, z, last(qrs[:, t, :], HD), ALU.mult)
                    tt(z, z, qkgain, ALU.mult, "qk_ready")
                    if t:
                        zz = z.rearrange("p u (b x c) -> p u b x c", b=2, x=2)
                        sc = scratch.rearrange("p u (b x c) -> p u b x c", b=2, x=2)
                        sn = early[:, EARLY["sin"]].rearrange("p (t b x c) -> p t b x c", t=2, b=2, x=2)
                        cs = early[:, EARLY["cos"]].rearrange("p (t c) -> p t c", t=2)
                        for b in range(2):
                            for y in range(2):
                                tt(sc[:, :, b, y, :], zz[:, :, b, 1 - y, :], lead(sn[:, t - 1, b, y, :], QK_HEADS),
                                   ALU.mult)
                        tt(z, z, lead(cs[:, t - 1, :], QK_HEADS), ALU.mult)
                        tt(z, z, scratch, ALU.add)

            def copy_b_keys():
                for t in range(NT):
                    v.wait_ge(S["bt_done"], 2 * t + 2)
                    cp(bkT[:, :, t * P:t * P + P], banks[4][:, :].rearrange("p (u s) -> p u s", u=4), "bt_copied_k")

            def mlstm():
                v.wait_ge(S["cum_done"], 1)
                sums = banks[0][:, 0:48].rearrange("p (s c) -> p s c", s=3)
                cp(bcum[:, :, :], sums[:, :, 0:8])
                cp(btot[:, :, :], sums[:, :, 8:16])
                tt(rrow[:, :, :], li[:, :, :], bcum[:, :, :], ALU.subtract, "rrow_ready")

                def exponents(s):
                    v.wait_ge(S["rows_done"], s + 1)
                    w, ex = wexp[s % 2], expo[s % 2]
                    for d in range(2):
                        R = banks[1 + d][:, :].rearrange("p (u s) -> p u s", u=4)
                        red(gall[:, 4 * d:4 * d + 4], R, ALU.max)
                        tt(w[:, 4 * d:4 * d + 4, :], R, lead(early[:, EARLY["maskb" if d else "maskf"]], 4), ALU.add)
                    red(gcol[:, :], w, ALU.max)
                    tt(gcol[:, :], gcol[:, :], mstate[:, :], ALU.max)
                    tt(gpick[:, :], gall[:, :], mstate[:, :], ALU.max)
                    tt(ex[:, 0, :], mstate[:, :], gcol[:, :], ALU.subtract)
                    tt(ex[:, 1, :], bcum[:, s, :], gcol[:, :], ALU.add)
                    ts(ex[:, 1, :], ex[:, 1, :], -1.0, None, ALU.mult)
                    tt(ex[:, 2, :], rrow[:, s, :], gpick[:, :], ALU.subtract)
                    tt(ex[:, 3, :], mstate[:, :], gpick[:, :], ALU.subtract, "expo_ready")
                    tt(w, w, last(gcol[:, :], P), ALU.subtract, "wexp_ready")
                    if s == 0:
                        tt(mout[:, :], btot[:, 0, :], gpick[:, :], ALU.add)
                        v.wait_ge(S["small_loaded"], 16 * 6)
                        cp(mstate[:, :], m0)
                    if s == 1:
                        tt(mstate[:, :], btot[:, 1, :], gpick[:, :], ALU.add)

                def combine_heads(s, d):
                    t, w, ex = STAGES[s][d], 2 * s + d, expo[s % 2]
                    heads = slice(4 * d, 4 * d + 4)
                    v.wait_ge(S["sums_done"], s + 1)
                    if s > 0:
                        tt(den[:, :], banks[1][:, 4 * d:4 * d + 4], ex[:, 0, heads], ALU.mult)
                        tt(den[:, :], den[:, :], dena[:, heads], ALU.add)
                    else:
                        cp(den[:, :], dena[:, heads])
                    stt(den[:, :], den[:, :], -1.0, den[:, :], ALU.mult, ALU.max)
                    tt(den[:, :], den[:, :], ex[:, 1, heads], ALU.max)
                    do(v.reciprocal(den[:, :], den[:, :]))
                    v.wait_ge(S["bnum_done"], w + 1)
                    num = banks[5][:, :].rearrange("p (u s) -> p u s", u=4)
                    if s > 0:
                        tt(tmp1, banks[6][:, :].rearrange("p (u s) -> p u s", u=4), last(ex[:, 0, heads], P), ALU.mult)
                        tt(tmp1, tmp1, num, ALU.add)
                        num = tmp1
                    out = hm[:, t, :].rearrange("p (u s) -> p u s", u=4)
                    first = (s == 0 and d == 0) or s == 1
                    if first:
                        tt(out, num, last(den[:, :], BD), ALU.mult, "combined")
                    else:
                        tt(tmp1, num, last(den[:, :], BD), ALU.mult)
                        tt(out, out, tmp1, ALU.add, "combined")

                def update_state(s, d):
                    heads = slice(4 * d, 4 * d + 4)
                    v.wait_ge(S["bupd_done"], 2 * s + d + 1)
                    upd = banks[(3, 0)[d]][:, :].rearrange("p (u s) -> p u s", u=4)
                    nup = banks[2][:, heads]
                    if s == 0:
                        cp(nout[:, heads], nup)
                        cp(Cout[:, heads, :], upd, "cstate_ready")
                    else:
                        decay = expo[s % 2][:, 3, heads]
                        tt(Cst[:, heads, :], Cst[:, heads, :], last(decay, P), ALU.mult)
                        tt(nst[:, heads], nst[:, heads], decay, ALU.mult)
                        tt(nst[:, heads], nst[:, heads], nup, ALU.add)
                        tt(Cst[:, heads, :], Cst[:, heads, :], upd, ALU.add, "cstate_ready")

                exponents(0)
                for s in range(3):
                    v.wait_ge(S["wexp_done"], s + 1)
                    for d in range(2):
                        heads = slice(4 * d, 4 * d + 4)
                        v.wait_ge(S["bs_done"], 2 * s + d + 1)
                        stt(amat[d].rearrange("p u s -> p (u s)"), banks[(3, 0)[d]][:, :], BD ** -0.5,
                            wexp[s % 2][:, heads, :].rearrange("p u s -> p (u s)"), ALU.mult, ALU.mult, "amat_ready")
                        if s < 2:
                            kk = qkv[0][:, STAGES[s][d], BK:BK + 512].rearrange("p (u s) -> p u s", u=4)
                            stt(kw[d], kk, BD ** -0.5, last(expo[s % 2][:, 2, heads], P), ALU.mult, ALU.mult,
                                "kw_ready")
                        red(dena[:, heads], amat[d], ALU.add)
                    if s < 2:
                        exponents(s + 1)
                    else:
                        duplicate_keys()
                    for d in range(2):
                        if s == 1 and d == 0:
                            v.wait_ge(S["state_loaded"], 48)
                        combine_heads(s, d)
                        if s < 2:
                            update_state(s, d)
                    if s:
                        modulation(2 + s)
            def mixer_b_squares(t):
                out = hm[:, t, :].rearrange("p (u s) -> p u s", u=4)
                tt(tmp1, out, out, ALU.mult)
                red(hss[:, t, :], tmp1, ALU.add, "dve_step" if t < NT - 1 else "hm_squares")

            def mixer_b_out(t):
                if t == 0:
                    v.wait_ge(S["hm_rooted"], 1)
                    do(v.reciprocal(hss[:, :, :], hss[:, :, :]))
                out = hm[:, t, :].rearrange("p (u s) -> p u s", u=4)
                dst = qkv[0][:, t, BQ:BQ + 512].rearrange("p (u s) -> p u s", u=4)
                tt(tmp1, out, last(hss[:, t, :], BD), ALU.mult)
                tt(tmp1, tmp1, ogain, ALU.mult)
                v.wait_ge(S["ogate_done"], t + 1)
                tt(dst, tmp1, qkv[0][:, t, BO:BO + 512].rearrange("p (u s) -> p u s", u=4), ALU.mult, "bout_ready")

            def duplicate_keys():
                for g in range(A_KV):
                    for s in range(4):
                        src = ctx_kv[:, 0, g * HD:g * HD + HD] if s == 1 else \
                            qkv[0][:, (0, None, 1, 2)[s], AK + g * HD:AK + g * HD + HD]
                        cp(kdup[:, g, s, :, :], lead(src, 2), "dve_step" if g * 4 + s < 7 else "kdup_ready")

            def window_bias():
                v.wait_ge(S["bias_loaded"], 16 * 2 * C_HEADS)
                for hh in range(C_HEADS):
                    tt(bias_na[:, hh, :, :], bias_na[:, hh, :, :], lead(keep[:, KEEP["window"]], 6), ALU.add,
                       "dve_step" if hh < C_HEADS - 1 else "bias_ready")

            def attention(l):
                def copy_keys(j):
                    g = (0, NP[0])[l] + j
                    v.wait_ge(S["pair_done"], 2 * g + 2)
                    if j >= 2:
                        v.wait_ge(S["scores_done"], U0[l] + NT * (j - 1))
                    cp(kT[l][:, g % 2, :], banks[7][:, :], "kT_copied")

                copy_keys(0)
                for i in range(NU[l] + 3):
                    if i >= 3:
                        j, t = unit(i - 3)
                        U = U0[l] + i - 3
                        v.wait_ge(S["pv_done"], U + 1)
                        col = 2 * (U % 4)
                        do(v.reciprocal(rlsum[:, col:col + 2], lsum[:, col:col + 2]))
                        c0 = 2 * j * HD
                        tt(qkv[l][:, t, c0:c0 + 2 * HD].rearrange("p (x c) -> p x c", x=2),
                           banks[6][:, 0:2 * HD].rearrange("p (x c) -> p x c", x=2),
                           last(rlsum[:, col:col + 2], HD), ALU.mult, "heads_out")
                    if i < NU[l]:
                        j, t = unit(i)
                        U = U0[l] + i
                        k0, k1 = keys_of(t)
                        v.wait_ge(S["scores_done"], U + 1)
                        col = 2 * (U % 4)
                        do(v.tensor_reduce(negm[:, col:col + 2], psum[:, 2 * (U % 2):2 * (U % 2) + 2, 0:k1 - k0], AX,
                                           ALU.max, negate=True), "max_ready")
                    if i % NT == 1 and i // NT + 1 < NP[l]:
                        copy_keys(i // NT + 1)
                    if l == 0 and 2 <= i < 2 + NT:
                        mixer_b_squares(i - 2)
                    if l == 0 and 7 <= i < 7 + NT:
                        mixer_b_out(i - 7)
                    if l == 0 and i == 10:
                        modulation(5)

            def mix_in(l, t):
                if t == 0:
                    v.wait_ge(S["modG_loaded"], 16 * (2 * l + 1))
                for c in range(OUT_CHUNKS):
                    g = l * NT * OUT_CHUNKS + t * OUT_CHUNKS + c
                    cond = 0 if t == 0 else 1
                    v.wait_ge(S["out_done"], g + 1)
                    cols = slice(512 * c, 512 * c + 512)
                    tt(mixed[:, c, :], banks[2 + g % 2][:, :], modG[:, cond, cols], ALU.mult)
                    tt(x[:, t, cols], x[:, t, cols], mixed[:, c, :], ALU.add, "x_mixed")

            rbias = rbias_sb[:, :]
            m0 = m0_sb[:, :]
            r3 = lambda o, n: rt[:, o:o + 3 * n].rearrange("p (t n) -> p t n", t=NT)
            chosen, g4, d3 = r3(0, 32), r3(96, 4), rt[:, 108:111]
            lg, cg, og = r3(120, 36), r3(228, 4), r3(240, 4)
            gm, mn, gp = rt[:, 252:255], rt[:, 255:258], rt[:, 258:261]
            em, c32, o1, o2 = r3(264, 32), r3(360, 32), r3(456, 32), r3(552, 32)
            m1, m2, sl, fin2 = rt[:, 648:651], rt[:, 651:654], r3(656, 32), rt[:, 752:752 + OVER]
            cnt, ex, ia, ib = rt[:, 760:792], rt[:, 792:824], rt[:, 824:856], rt[:, 856:888]
            iota = keep[:, KEEP["slot"]][:, 0:32]

            def route(l):
                def first_of(eq, width, onehot, top, logits):
                    tt(eq, logits, last(top, width), ALU.is_equal)
                    stt(eq, eq, -1000.0, lead(iota[:, 0:width], NT), ALU.mult, ALU.add)
                    red(mn, eq, ALU.min)
                    tt(onehot, eq, last(mn, width), ALU.is_equal)

                v.wait_ge(S["logits_done"], l + 1)
                v.wait_ge(S["kv_stored"], 32 * (l + 1))
                v.wait_ge(S["wge_loaded"], 32 * (l + 1))
                tt(lg, banks[6][:, 0:108].rearrange("p (t n) -> p t n", t=NT), lead(rbias, NT), ALU.add)
                red(gm, lg[:, :, 0:4], ALU.max)
                tt(g4, lg[:, :, 0:4], last(gm, 4), ALU.subtract, "route_exp")
                first_of(cg, 4, og, gm, lg[:, :, 0:4])
                ts(cg, og, FAR, -FAR, ALU.mult, ALU.add)
                for t in range(NT):
                    le = lg[:, t, 4:36].rearrange("p (g e) -> p g e", g=GROUPS)
                    emt = em[:, t, :].rearrange("p (g e) -> p g e", g=GROUPS)
                    tt(emt, le, last(og[:, t, :], PER_GROUP), ALU.mult)
                    tt(emt, emt, last(cg[:, t, :], PER_GROUP), ALU.add)
                red(m1, em, ALU.max)
                first_of(c32, 32, o1, m1, em)
                stt(em, o1, -3.0 * FAR, em, ALU.mult, ALU.add)
                red(m2, em, ALU.max)
                first_of(c32, 32, o2, m2, em)
                tt(chosen, o1, o2, ALU.add, "chosen")
                tt(d3, m2, m1, ALU.subtract, "route_exp")
                stt(val, o2, 2.0, last(keep[:, KEEP["pair"]], EXPERTS), ALU.mult, ALU.add)
                for k in range(2):
                    ts(pval[:, k, :], keep[:, KEEP["pair"]], 2.0 * k, None, ALU.add)
                v.wait_ge(S["ranks_done"], l + 1)
                tt(sl, banks[2][:, 0:96].rearrange("p (t n) -> p t n", t=NT), chosen, ALU.mult)
                cp(cnt, banks[2][:, 96:128])
                ts(key, sl, -1.0, None, ALU.add, name="chosen_keys")

            def weigh(l):
                v.wait_ge(S["route_exped"], 2 * l + 2)
                red(gp, g4, ALU.add)
                stt(gm, d3, 1.0, gp, ALU.add, ALU.mult)
                do(v.reciprocal(wtop[:, :, 0], gm))
                tt(wtop[:, :, 1], wtop[:, :, 0], d3, ALU.mult)
                ts(ex, cnt, float(BLOCK), None, ALU.is_gt)
                for m in range(2, TOKENS // BLOCK):
                    stt(ex, cnt, float(BLOCK * m), ex, ALU.is_gt, ALU.add)
                cp(ia, ex)
                src, dst = ia, ib
                for sh in (1, 2, 4, 8, 16):
                    cp(dst[:, 0:sh], src[:, 0:sh])
                    tt(dst[:, sh:32], src[:, sh:32], src[:, 0:32 - sh], ALU.add)
                    src, dst = dst, src
                tt(dst, src, ex, ALU.subtract)
                ts(dst, dst, float(BLOCK), -float(BLOCK), ALU.mult, ALU.add)
                ts(c32, key, float(BLOCK), SKIP, ALU.is_lt, ALU.mult)
                tt(em, key, lead(dst, NT), ALU.add)
                tt(em, em, c32, ALU.subtract)
                for k, oh in enumerate((o1, o2)):
                    tt(oh, oh, em, ALU.mult)
                    red(m1, oh, ALU.add)
                    for t in range(NT):
                        stt(okey[:, k, t, :], iota[:, 0:OVER + 1], -float(BLOCK), m1[:, t:t + 1].to_broadcast([P, OVER + 1]),
                            ALU.mult, ALU.add)
                grid = rt[:, 264:264 + OVER * 32].rearrange("p (b e) -> p b e", b=OVER)
                tt(grid, lead(src, OVER), last(iota[:, 0:OVER], 32), ALU.is_le)
                red(fin2, grid, ALU.add)
                ts(eid_i[:, 0:OVER], fin2, float(EXPERTS - 1), None, ALU.min)
                cp(eid_i[:, OVER:OVER + 1], src[:, 31:32], "over_ready")

            def one(e, u, base):
                def old(name):
                    if not (isinstance(e, int) and e + base < 2):
                        v.wait_ge(M[name], e + (base - 1))

                v.wait_ge(M["hid_done"], e + (base + 1))
                old("hidT_done")
                v.tensor_copy(hs[u][64:128, :], banks[2 + u][64:128, :]).then_inc(M["up_copied"], 1)

            def tokens(e, u, base):
                v.wait_ge(M["xT_done"], e + (base + 1))
                if not (isinstance(e, int) and e + base < 2):
                    v.wait_ge(M["hid_done"], e + (base - 1))
                v.tensor_copy(xT[u][:, :, :].rearrange("p k s -> p (k s)"), banks[1][:, :]).then_inc(M["xT_copied"], 1)

            def pick(e, u, base):
                if not (isinstance(e, int) and e < 2):
                    v.wait_ge(M["index_done"], e + (base - 1))
                rank = key[:, :, e] if isinstance(e, int) else key[:, :, bass.ds(e, 1)].rearrange("p t e -> p (t e)")
                v.tensor_tensor(sel[u], lead(keep[:, KEEP["slot"]], NT), last(rank, P), ALU.is_equal)\
                    .then_inc(M["sel_ready"], 1)

            def index(e, u, base):
                v.wait_ge(M["index_done"], e + (base + 1))
                if not (isinstance(e, int) and e + base < 2):
                    v.wait_ge(M[f"scattered{u}"], scat(e, u, base) - 16)
                v.tensor_scalar(idx[u][:, :], banks[5][:, 0:1], keep[:, KEEP["skip"]], None, ALU.add)\
                    .then_inc(M["index_ready"], 1)

            def product(e, u, base):
                v.wait_ge(M["upT_copied"], e + (base + 1))
                if not (isinstance(e, int) and e + base < 2):
                    v.wait_ge(M["y_done"], e + (base - 1))
                v.tensor_tensor(hidT[u][:, :, :], banks[4][:, :].rearrange("p (k n) -> p k n", k=4)[:, :, 0:64],
                                upT[u][:, :, :], ALU.mult).then_inc(M["hidT_ready"], 1)

            def experts(l):
                base = l * EXPERTS

                def whole(e, u, lasts=2):
                    one(e, u, base)
                    product(e, u, base)
                    if lasts:
                        tokens(e + 1, 1 - u, base)
                        index(e + 1, 1 - u, base)
                    if lasts > 1:
                        pick(e + 2, u, base)

                pick(0, 0, base)
                pick(1, 1, base)
                tokens(0, 0, base)
                index(0, 0, base)
                whole(0, 0)
                weigh(l)
                whole(1, 1)
                with v.Fori(1, EXPERTS // 2 - 1) as i:
                    for u in range(2):
                        whole(v.snap(i * 2 + u), u)
                whole(EXPERTS - 2, 0, 1)
                whole(EXPERTS - 1, 1, 0)
                v.wait_ge(S["over_ready"], l + 1)
                n_over = v.value_load(eid_i[0:1, OVER:OVER + 1], min_val=0, max_val=OVER)
                V = OV[l]

                def pick_over(b):
                    for k in range(2):
                        rank = okey[:, k, :, b] if isinstance(b, int) else \
                            okey[:, k, :, bass.ds(b, 1)].rearrange("p t b -> p (t b)")
                        ins = v.tensor_tensor(sel[k], lead(keep[:, KEEP["slot"]], NT), last(rank, P), ALU.is_equal)
                    ins.then_inc(V["sel_ready"], 1)

                with v.If(n_over > 0):
                    pick_over(0)
                    with v.Fori(0, OVER) as b:
                        v.wait_ge(V["xT_done"], b + 1)
                        v.tensor_copy(xT[0][:, :, :].rearrange("p k s -> p (k s)"), banks[1][:, :])\
                            .then_inc(V["xT_copied"], 1)
                        v.wait_ge(V["index_done"], b + 1)
                        v.tensor_scalar(idx[0][:, :], banks[5][:, 0:1], keep[:, KEEP["skip"]], None, ALU.add)\
                            .then_inc(V["index_ready"], 1)
                        v.wait_ge(V["hid_done"], b + 1)
                        v.tensor_copy(hs[0][64:128, :], banks[2][64:128, :]).then_inc(V["hs_ready"], 1)
                        v.wait_ge(V["upT_copied"], b + 1)
                        v.tensor_tensor(hidT[0][:, :, :],
                                        banks[4][:, :].rearrange("p (k n) -> p k n", k=4)[:, :, 0:64],
                                        upT[0][:, :, :], ALU.mult).then_inc(V["hidT_ready"], 1)
                        v.wait_ge(V["scattered0"], b * 16 + 16)
                        pick_over(v.snap(b + 1))

            def combine(l, t):
                if t == 0:
                    v.wait_ge(S["modG_loaded"], 16 * (2 * l + 2))
                c = 0 if t == 0 else 1
                v.wait_ge(S["pair_scaled"], NT * l + t + 1)
                y = pairs[:, t, 0, :]
                stt(y, pairs[:, t, 1, :], wtop[:, t, 1:2], y, ALU.mult, ALU.add)
                tt(y, y, modG[:, c, :], ALU.mult)
                tt(x[:, t, :], x[:, t, :], y, ALU.add, "x_moe")

            def rows(step, idx, behind):
                for t in range(NT + behind):
                    if t < NT:
                        step(t)
                    if t >= behind:
                        normed(idx, t - behind)

            first_modulation()
            for t in range(NT):
                normed(0, t)
            for l in range(2):
                copy_projected(l)
                if l == 0:
                    gate_logs()
                    mlstm()
                attention(l)
                rows(lambda t: mix_in(l, t), 2 * l + 1, 0)
                route(l)
                experts(l)
                rows(lambda t: combine(l, t), 2 * l + 2, 1)

        @block.gpsimd
        def _(pool):
            def get(dst, src, name, tiny=False):
                pool.dma_start(dst, src, allow_slow_non_contiguous=tiny).then_inc(S[name], 16)

            def spread(ap, n=P):
                return ap.unsqueeze(0).to_broadcast([n] + list(ap.shape))

            def store_ada(l, g):
                G = 3 * l + g
                pool.wait_ge(S["ada_copied"], G + 1)
                dst = mod_dram[l].rearrange("c (v j n) -> c v j n", v=ADA_CHUNKS, j=4)
                for j in range(4):
                    pool.dma_start(dst[:, 4 * g:4 * g + 4, j, :], modsb[32 * j:32 * j + 32:16, G % 2, :, :])\
                        .then_inc(S[f"ada_stored{G % 2}"], 16)

            def finish_mod(G):
                l, g = divmod(G, 3)
                pool.wait_ge(S[f"ada_stored{G % 2}"], stored(G))
                if G >= 3:
                    pool.wait_ge(S["cmod_stored"], 32 * (G - 2))
                for c in range(2):
                    get(cmod[:, G % 2, c, :, :],
                        mod_dram[l, c].rearrange("(v p i) -> p v i", v=6, p=P)[:, 2 * g:2 * g + 2, :], "cmod_loaded")
                pool.wait_ge(S["cmod_ready"], G)
                for c in range(2):
                    get(modf_dram[l, 2 * g:2 * g + 2, c, :].rearrange("v (p i) -> p v i", p=P),
                        cmod[:, G % 2, c, :, :], "cmod_stored")

            def load_AB(l, which):
                get(modA[:, :, :], spread(modf_dram[l, 3 * which + 1]), "modAB_loaded")
                get(modB[:, :, :], spread(modf_dram[l, 3 * which]), "modAB_loaded")

            def load_G(l, which):
                get(modG[:, :, :], spread(modf_dram[l, 3 * which + 2]), "modG_loaded")

            get(keep[:, :], a["keep"], "keep_loaded")
            get(bias_row, a["ada_b"][0, 0:2 * D].unsqueeze(0), "bias_row_loaded")
            get(x[:, 0, :], a["x_prompt"][0], "x_loaded")
            get(x[:, 1:NT, :], a["x_sample"][0].rearrange("(t p) d -> p t d", p=P), "x_rest")
            get(first_gain, spread(a["norm_mix"][0]), "first_gain_loaded")
            for l in range(2):
                get(cada[:, l, :, :], a["ada_b"][l].rearrange("(v p i) -> p v i", v=6, p=P), "cgain_loaded")
                get(cgain[:, l, 0, :], a["norm_mix"][l].rearrange("(p i) -> p i", p=P), "cgain_loaded")
                get(cgain[:, l, 1, :], a["norm_ffn"][l].rearrange("(p i) -> p i", p=P), "cgain_loaded")
            get(early, a["early"], "early_loaded")
            pool.wait_ge(S["h_ready"], NT)
            gv = a["ab_q_norm"][0]
            get(qkgain[:, 0:A_HEADS, :], gv.unsqueeze(0).unsqueeze(0).to_broadcast([P, A_HEADS, HD]), "small_loaded")
            get(qkgain[:, A_HEADS:QK_HEADS, :],
                a["ab_k_norm"][0].unsqueeze(0).unsqueeze(0).to_broadcast([P, A_KV, HD]), "small_loaded")
            get(gbias, spread(a["ab_gate_bias"][0].rearrange("g h -> (g h)")), "small_loaded")
            get(ogain, spread(a["ab_out_norm"][0]), "small_loaded")
            get(m0_sb[:, :], spread(a["state_mlstm_m"][0, 0].rearrange("d h -> (d h)")), "small_loaded")
            for v2, src in enumerate((a["cache_attn_k"], a["cache_attn_v"])):
                get(ctx_kv[:, v2, :], src[0, 0].rearrange("t g d -> t (g d)"), "small_loaded" if v2 == 0 else "ctx_v")
            get(Cst[:, 0:4, :], a["state_mlstm_C"][0, 0, 0].rearrange("h d e -> d h e"), "state_loaded")
            get(Cst[:, 4:8, :], a["state_mlstm_C"][0, 0, 1].rearrange("h d e -> d h e"), "state_loaded")
            get(nst[:, :], a["state_mlstm_n"][0, 0].rearrange("d h e -> e (d h)"), "state_loaded", True)
            for G in range(1, 4):
                store_ada(*divmod(G, 3))
                finish_mod(G)
            pool.wait_ge(S["qk_ready"], 1)
            for dst, c0 in ((o["new_attn_k"], AK), (o["new_attn_v"], AV)):
                get(dst[0, 0].rearrange("t g d -> t (g d)"), qkv[0][:, 0, c0:c0 + A_KV * HD], "kv_stored")
            pool.wait_ge(S["cstate_ready"], 2)
            get(o["new_mlstm_C"][0, 0].rearrange("d h e f -> e (d h) f"), Cout[:, :, :], "state_stored")
            get(o["new_mlstm_n"][0, 0].rearrange("d h e -> e (d h)"), nout[:, :], "state_stored", True)
            get(o["new_mlstm_m"][0, 0].rearrange("d h -> (d h)").unsqueeze(0), mout[0:1, :], "state_stored")
            for G in range(4, 6):
                store_ada(*divmod(G, 3))
                finish_mod(G)
            pool.wait_ge(S["state_stored"], 48)

            def scatter(Q, e, u, base, l):
                pool.wait_ge(Q["y_copied"], e + (base + 1))
                pool.indirect_dma_start(out=pair_dram[l], in_=ysb[u], in_offset=None,
                                        out_offset=bass.IndirectOffsetOnAxis(ap=idx[u][:, :], axis=0),
                                        bounds_check=2 * PAIRS - 1, oob_is_err=False)\
                    .then_inc(Q[f"scattered{u}"], 16)

            for l in range(2):
                if l == 1:
                    pool.wait_ge(S["h_ready"], NT * 3)
                    for hh in range(C_HEADS):
                        for rr in range(2):
                            src = bass.AP(a["rpb"].tensor, (hh * 7 + 1 - rr) * 127, [[1, GRID_W], [127, 6], [1, GRID_W]])
                            get(bias_na[64 * rr:64 * rr + 64, hh, :, :], src, "bias_loaded")
                    pool.wait_ge(S["trans_done"], 2 * NT * 3)
                    get(na_k, a["cache_na_k"][0, 0].rearrange("t h d -> t (h d)"), "na_ctx_loaded")
                    pool.wait_ge(S["proj_done"], PROJ0[1] + NA_CHUNKS * NT)
                    get(na_v, a["cache_na_v"][0, 0].rearrange("t h d -> t (h d)"), "na_v_loaded")
                    for name in ("proj_copied_dve", "proj_copied_act"):
                        pool.wait_ge(S[name], (PROJ0[1] + NA_CHUNKS * NT) // 2)
                    for dst, c0 in ((o["new_na_k"], D), (o["new_na_v"], 2 * D)):
                        get(dst[0, 0].rearrange("t h d -> t (h d)"), qkv[1][:, 0, c0:c0 + D], "kv_stored")
                pool.wait_ge(S["heads_out"], U0[l] + NU[l])
                if l == 0:
                    pool.wait_ge(S["cmod_stored"], 160)
                load_G(l, 0)
                load_AB(l, 1)
                wv = a["moe_wg"][l].rearrange("(k p) n -> p k n", p=P)
                get(wge[:, :, 0:GROUPS], wv, "wge_w")
                get(wge[:, :, GROUPS:], a["moe_we"][l].rearrange("(k p) n -> p k n", p=P), "wge_w")
                get(rbias_sb[:, 0:GROUPS], spread(a["moe_bg"][l]), "wge_loaded")
                get(rbias_sb[:, GROUPS:], spread(a["moe_be"][l]), "wge_loaded")
                pool.wait_ge(S["x_mixed"], NT * OUT_CHUNKS * (l + 1))
                load_G(l, 1)
                pool.wait_ge(S["h_ready"], NT * (2 * l + 2))
                if l == 0:
                    load_AB(1, 0)
                else:
                    get(modA[:, 0, :], spread(a["norm_final"]), "gfin_loaded")
                base = l * EXPERTS
                for e in range(EXPERTS):
                    scatter(M, e, e % 2, base, l)
                pool.wait_ge(S["over_ready"], l + 1)
                n_over = pool.value_load(eid_i[0:1, OVER:OVER + 1], min_val=0, max_val=OVER)
                with pool.If(n_over > 0):
                    for b in range(OVER):
                        scatter(OV[l], b, 0, 0, l)
                        pool.wait_ge(OV[l]["scattered0"], 16 * (b + 1))
                    pool.wait_ge(OV[l]["sel_ready"], OVER + 1)
                for u in range(2):
                    pool.wait_ge(M[f"scattered{u}"], 16 * (l + 1) * EXPERTS // 2)
                for t in range(NT):
                    get(pairs[:, t, :, :].rearrange("p k d -> p (k d)"),
                        pair_dram[l].rearrange("(t p c) d -> t p (c d)", t=NT, p=P)[t], f"pairs_loaded{t}")
            for t in range(NT):
                pool.wait_ge(S["y_ready"], t + 1)
                dst = o["y_prompt"][0] if t == 0 else o["y_sample"][0, (t - 1) * P:t * P, :]
                get(dst, h[:, t, :], "y_stored")
            pool.wait_ge(S["y_stored"], 16 * NT)
            pool.wait_ge(S["kv_stored"], 64)
            pool.wait_ge(S["state_stored"], 48)


_OUTS = [("y_prompt", (1, SEQ, D)), ("y_sample", (1, DEC_SEQ, D)), ("new_attn_k", (1, 1, SEQ, A_KV, HD)),
         ("new_attn_v", (1, 1, SEQ, A_KV, HD)), ("new_mlstm_C", (1, 1, 2, B_HEADS, BD, BD)),
         ("new_mlstm_n", (1, 1, 2, B_HEADS, BD)), ("new_mlstm_m", (1, 1, 2, B_HEADS)),
         ("new_na_k", (1, 1, SEQ, C_HEADS, HD)), ("new_na_v", (1, 1, SEQ, C_HEADS, HD))]


def kernel(**inputs):
    import concourse.bacc as _bacc
    from concourse.bass_utils import run_bass_kernel_spmd as _run

    nc = _bacc.Bacc("TRN2", target_bir_lowering=False, num_devices=1)
    arrays, aps = {}, {}
    inputs = {k: np.asarray(v) for k, v in inputs.items()}
    rpb = inputs.pop("na_rpb")[0]
    reach = ROWS - 1
    padded = np.zeros((C_HEADS, 2 * ROWS - 1, 2 * GRID_W - 1), rpb.dtype)
    mid = GRID_W - NA_COLS
    padded[:, :, mid:mid + 2 * NA_COLS - 1] = rpb[:, NA_ROWS_MAX - 1 - reach:NA_ROWS_MAX + reach]
    inputs["rpb"] = padded
    inputs["keep"], inputs["early"] = tables()
    for name, value in inputs.items():
        value = np.ascontiguousarray(value)
        arrays[f"in_{name}"] = value
        aps[name] = nc.dram_tensor(f"in_{name}", value.shape, mybir.dt.from_np(value.dtype), kind="ExternalInput").ap()
    outs = {n: nc.dram_tensor(f"out_{n}", s, F32, kind="ExternalOutput").ap() for n, s in _OUTS}
    build(nc, aps, outs)
    r = _run(nc, [arrays], core_ids=[0])
    return tuple(r.results[0][f"out_{n}"] for n, _ in _OUTS)
```
